# Optimizing a Trainium2 kernel written in Bass

```python
import math
import jax, jax.numpy as jnp
from jax import lax
import numpy as np

D_MODEL = 1024
BATCH = 1
SEQ = 256
DEPTH = 2

N_HEADS = 8
N_KV_HEADS = 2
HEAD_DIM = 64
GQA_GROUP = N_HEADS // N_KV_HEADS
WINDOW = 128
ATTN_BLOCK = WINDOW
Q_DIM = N_HEADS * HEAD_DIM
KV_DIM = N_KV_HEADS * HEAD_DIM
N_BUCKETS = 32
MAX_DISTANCE = 128
POOL_WINDOWS = (2, 4, 8, 16)
POOL_GROUPS = 4
POOL_GROUP_DIM = 128
POOL_DIM = POOL_GROUPS * POOL_GROUP_DIM
GMLP_CHUNK = 128
GMLP_GROUPS = 4
GMLP_DIM = 512
GMLP_GROUP_DIM = GMLP_DIM // GMLP_GROUPS
N_BRANCHES = 3
GATE_DIM = N_BRANCHES * D_MODEL
SPLIT_POINTS = (Q_DIM, Q_DIM + KV_DIM, Q_DIM + 2 * KV_DIM, Q_DIM + 2 * KV_DIM + POOL_DIM, Q_DIM + 2 * KV_DIM + POOL_DIM + GMLP_DIM, Q_DIM + 2 * KV_DIM + POOL_DIM + 2 * GMLP_DIM)
IN_DIM = Q_DIM + 2 * KV_DIM + POOL_DIM + 2 * GMLP_DIM + GATE_DIM
PEER_HEADS = 8
N_KEYS = 128
N_EXPERTS = N_KEYS * N_KEYS
PEER_TOPK = 16
PEER_QDIM = 256
PEER_HALF = PEER_QDIM // 2
PEER_BLOCK = 128
EPS = 1e-6
NEG_INF = -1e30

kernel_name = "hybrid_gated_swa_pool_gmlp_peer"

def rmsnorm(x, gain):
    xf = x.astype(jnp.float32)
    y = xf * lax.rsqrt(jnp.mean(xf * xf, axis=-1, keepdims=True) + EPS)
    return (y * gain.astype(jnp.float32)).astype(x.dtype)

def t5_causal_bucket(dist):
    n = jnp.maximum(dist, 0)
    max_exact = N_BUCKETS // 2
    nf = jnp.maximum(n, 1).astype(jnp.float32)
    large = max_exact + (jnp.log(nf / max_exact) / math.log(MAX_DISTANCE / max_exact) * (N_BUCKETS - max_exact)).astype(jnp.int32)
    large = jnp.minimum(large, N_BUCKETS - 1)
    return jnp.where(n < max_exact, n, large)

def sliding_window_attention(q, k, v, sinks, rel_bias):
    B, S, _ = q.shape
    nb = S // ATTN_BLOCK
    q = q.reshape(B, nb, ATTN_BLOCK, N_KV_HEADS, GQA_GROUP, HEAD_DIM)
    k = k.reshape(B, nb, ATTN_BLOCK, N_KV_HEADS, HEAD_DIM)
    v = v.reshape(B, nb, ATTN_BLOCK, N_KV_HEADS, HEAD_DIM)

    def with_prev(t):
        prev = jnp.pad(t, ((0, 0), (1, 0), (0, 0), (0, 0), (0, 0)))[:, :-1]
        return jnp.concatenate([prev, t], axis=2)

    kk, vv = with_prev(k), with_prev(v)
    logits = jnp.einsum('bnqhgd,bnshd->bnhgqs', q, kk).astype(jnp.float32) * (HEAD_DIM ** -0.5)
    qi = jnp.arange(ATTN_BLOCK)[:, None]
    kj = jnp.arange(2 * ATTN_BLOCK)[None, :]
    dist = qi + ATTN_BLOCK - kj
    band = (dist >= 0) & (dist < WINDOW)
    bias = rel_bias[t5_causal_bucket(dist)].astype(jnp.float32)
    bias = bias.transpose(2, 0, 1).reshape(N_KV_HEADS, GQA_GROUP, ATTN_BLOCK, 2 * ATTN_BLOCK)
    before_start = (jnp.arange(nb) == 0)[:, None, None] & (kj < ATTN_BLOCK)[None]
    mask = band[None] & ~before_start
    logits = jnp.where(mask[None, :, None, None], logits + bias, NEG_INF)
    sink = sinks.astype(jnp.float32).reshape(N_KV_HEADS, GQA_GROUP)[:, :, None, None]
    m = jnp.maximum(jnp.max(logits, axis=-1, keepdims=True), sink)
    p = jnp.exp(logits - m)
    p = p / (jnp.sum(p, axis=-1, keepdims=True) + jnp.exp(sink - m))
    out = jnp.einsum('bnhgqs,bnshd->bnqhgd', p.astype(v.dtype), vv)
    return out.reshape(B, S, Q_DIM)

def multiscale_pool(z, w_pool, pool_scale):
    B, S, _ = z.shape
    zg = z.astype(jnp.float32).reshape(B, S, POOL_GROUPS, POOL_GROUP_DIM)
    csum = jnp.cumsum(zg, axis=1)
    count = jnp.arange(1, S + 1, dtype=jnp.float32)
    outs = []
    for gi, w in enumerate(POOL_WINDOWS):
        c = csum[:, :, gi]
        lagged = jnp.pad(c, ((0, 0), (w, 0), (0, 0)))[:, :S]
        mean = (c - lagged) / jnp.minimum(count, float(w))[None, :, None]
        outs.append(mean - zg[:, :, gi])
    d = jnp.stack(outs, axis=2).astype(z.dtype)
    y = jnp.einsum('bsgc,gcd->bsgd', d, w_pool)
    return y.reshape(B, S, POOL_DIM) * pool_scale

def chunked_spatial_gating(u, v, v_gain, w_s, b_s):
    B, S, _ = u.shape
    u = jax.nn.gelu(u)
    v = rmsnorm(jax.nn.gelu(v), v_gain)
    nc = S // GMLP_CHUNK
    v = v.reshape(B, nc, GMLP_CHUNK, GMLP_GROUPS, GMLP_GROUP_DIM)
    causal = jnp.tril(jnp.ones((GMLP_CHUNK, GMLP_CHUNK), dtype=bool))
    w = jnp.where(causal[None], w_s, jnp.zeros_like(w_s))
    mixed = jnp.einsum('gts,bcsgd->bctgd', w, v) + b_s.T[:, :, None]
    return u * mixed.reshape(B, S, GMLP_DIM)

def peer_ffn(h, w_query, sub_keys1, sub_keys2, expert_u, expert_v):
    B, S, D = h.shape
    tokens = h.reshape(-1, PEER_BLOCK, D)

    def block(xb):
        q = (xb @ w_query).reshape(PEER_BLOCK, PEER_HEADS, 2, PEER_HALF)
        s1 = jnp.einsum('thd,kd->thk', q[:, :, 0], sub_keys1).astype(jnp.float32)
        s2 = jnp.einsum('thd,kd->thk', q[:, :, 1], sub_keys2).astype(jnp.float32)
        v1, i1 = lax.top_k(s1, PEER_TOPK)
        v2, i2 = lax.top_k(s2, PEER_TOPK)
        cand = (v1[..., :, None] + v2[..., None, :]).reshape(PEER_BLOCK, PEER_HEADS, PEER_TOPK * PEER_TOPK)
        top, ci = lax.top_k(cand, PEER_TOPK)
        idx = jnp.take_along_axis(i1, ci // PEER_TOPK, axis=-1) * N_KEYS + jnp.take_along_axis(i2, ci % PEER_TOPK, axis=-1)
        gate = jax.nn.softmax(top, axis=-1)
        idx = idx.reshape(PEER_BLOCK, PEER_HEADS * PEER_TOPK)
        gate = gate.reshape(PEER_BLOCK, PEER_HEADS * PEER_TOPK)
        u_sel = expert_u[idx]
        act = jax.nn.gelu(jnp.einsum('td,tkd->tk', xb, u_sel).astype(jnp.float32))
        coeff = (gate * act).astype(xb.dtype)
        return jnp.einsum('tk,tkd->td', coeff, expert_v[idx])

    return lax.map(block, tokens).reshape(B, S, D)

def setup_inputs(seed: int = 0) -> dict:
    key = jax.random.key(seed)
    ks = jax.random.split(key, 24)
    f32 = jnp.float32
    L, D = DEPTH, D_MODEL

    def nrm(k, shape, scale):
        return jax.random.normal(k, shape, f32) * scale

    return {
        "x": nrm(ks[0], (BATCH, SEQ, D), 1.0),
        "rel_bias": nrm(ks[1], (N_BUCKETS, N_HEADS), 0.5),
        "final_gain": 1.0 + nrm(ks[2], (D,), 0.02),
        "attn_norm_gain": 1.0 + nrm(ks[3], (L, D), 0.02),
        "w_in": nrm(ks[4], (L, D, IN_DIM), D ** -0.5),
        "b_gate": nrm(ks[5], (L, GATE_DIM), 0.02),
        "attn_sinks": nrm(ks[6], (L, N_HEADS), 0.5),
        "w_pool": nrm(ks[7], (L, POOL_GROUPS, POOL_GROUP_DIM, POOL_GROUP_DIM), POOL_GROUP_DIM ** -0.5),
        "pool_scale": 1.0 + nrm(ks[8], (L, POOL_DIM), 0.02),
        "gmlp_v_gain": 1.0 + nrm(ks[9], (L, GMLP_DIM), 0.02),
        "w_spatial": nrm(ks[10], (L, GMLP_GROUPS, GMLP_CHUNK, GMLP_CHUNK), GMLP_CHUNK ** -0.5),
        "b_spatial": 1.0 + nrm(ks[11], (L, GMLP_GROUPS, GMLP_CHUNK), 0.02),
        "w_branch_a": nrm(ks[12], (L, Q_DIM, D), Q_DIM ** -0.5),
        "w_branch_b": nrm(ks[13], (L, POOL_DIM, D), POOL_DIM ** -0.5),
        "w_branch_c": nrm(ks[14], (L, GMLP_DIM, D), GMLP_DIM ** -0.5),
        "w_out": nrm(ks[15], (L, D, D), D ** -0.5),
        "ffn_norm_gain": 1.0 + nrm(ks[16], (L, D), 0.02),
        "peer_w_query": nrm(ks[17], (L, D, PEER_HEADS * PEER_QDIM), D ** -0.5),
        "peer_sub_keys1": nrm(ks[18], (L, N_KEYS, PEER_HALF), PEER_HALF ** -0.5),
        "peer_sub_keys2": nrm(ks[19], (L, N_KEYS, PEER_HALF), PEER_HALF ** -0.5),
        "peer_expert_u": nrm(ks[20], (L, N_EXPERTS, D), D ** -0.5),
        "peer_expert_v": nrm(ks[21], (L, N_EXPERTS, D), PEER_HEADS ** -0.5),
    }

def reference(x, rel_bias, final_gain, attn_norm_gain, w_in, b_gate, attn_sinks, w_pool, pool_scale, gmlp_v_gain, w_spatial, b_spatial, w_branch_a, w_branch_b, w_branch_c, w_out, ffn_norm_gain, peer_w_query, peer_sub_keys1, peer_sub_keys2, peer_expert_u, peer_expert_v):
    B, S, D = x.shape
    for l in range(DEPTH):
        h = rmsnorm(x, attn_norm_gain[l])
        proj = h @ w_in[l]
        q, k, v, pz, gu, gv, g = jnp.split(proj, SPLIT_POINTS, axis=-1)
        gates = jax.nn.sigmoid((g + b_gate[l]).astype(jnp.float32)).astype(x.dtype).reshape(B, S, N_BRANCHES, D)
        ya = sliding_window_attention(q, k, v, attn_sinks[l], rel_bias) @ w_branch_a[l]
        yb = multiscale_pool(pz, w_pool[l], pool_scale[l]) @ w_branch_b[l]
        yc = chunked_spatial_gating(gu, gv, gmlp_v_gain[l], w_spatial[l], b_spatial[l]) @ w_branch_c[l]
        merged = gates[:, :, 0] * ya + gates[:, :, 1] * yb + gates[:, :, 2] * yc
        x = x + merged @ w_out[l]
        h2 = rmsnorm(x, ffn_norm_gain[l])
        x = x + peer_ffn(h2, peer_w_query[l], peer_sub_keys1[l], peer_sub_keys2[l], peer_expert_u[l], peer_expert_v[l])
    return rmsnorm(x, final_gain)


_drawn_inputs = setup_inputs


def setup_inputs(seed=0):
    import zlib

    import numpy as np

    out = dict(_drawn_inputs(seed))
    spreads = {}
    factors = {'final_gain': 2.777,
     'b_gate': 2.976,
     'attn_sinks': 4.851,
     'gmlp_v_gain': 3.179,
     'b_spatial': 2.674}
    for name, (base, spread) in spreads.items():
        noise = np.random.default_rng([zlib.crc32(name.encode()), seed]).standard_normal(out[name].shape)
        drawn = base * np.exp(spread * noise) if base else spread * noise
        out[name] = __import__('jax').numpy.asarray(drawn.astype(out[name].dtype))
    for name, factor in factors.items():
        out[name] = (out[name] * factor).astype(out[name].dtype)
    return out
```

```python
from contextlib import ExitStack

import numpy as np
import concourse.bass as bass
from concourse import mybir

F32 = mybir.dt.float32
U32 = mybir.dt.uint32
ALU = mybir.AluOpType
ACT = mybir.ActivationFunctionType
AX = mybir.AxisListType

P = 128
D = 1024
KD = D // P
S = 256
TT = S // P
DEPTH = 2
HEADS, HD = 8, 64
QC = HEADS * HD // P
WINDOW = 128
BUCKETS, MAX_DIST = 32, 128
GROUPS = 4
POOL_WINDOWS = (2, 4, 8, 16)
PAD = 16
BR = 3
PH, TOPK, NK = 8, 16, 128
HALF_N = 512
EPS = 1e-6
NEG = -1e30
LOW = -3e38

TILE = 1024
RING = 4
T_PARAM = 0
T_Q = T_PARAM + 2
T_K = T_Q + QC
T_V = T_K + 1
T_PZ = T_V + 1
T_GU = T_PZ + GROUPS
T_GV = T_GU + GROUPS
T_MIX = T_GV + 4
MIX_HALF = BR * 6
T_WO = T_MIX + 2 * MIX_HALF
T_WQ = T_WO + 8
T_UV = T_WQ + 2 * PH
NT = T_UV + 2 * NK
assert NT % RING == 0 and T_UV % RING == 0 and RING == 4

C_SK = 0
C_WPOOL = C_SK + 2 * NK
C_WSP = C_WPOOL + GROUPS * P
C_AGAIN = C_WSP + GROUPS * P
C_FGAIN = C_AGAIN + KD
C_BGATE = C_FGAIN + KD
C_PSCALE = C_BGATE + BR * KD
C_VGAIN = C_PSCALE + GROUPS
C_SINK = C_VGAIN + GROUPS
C_BSP = C_SINK + HEADS
C_END = C_BSP + GROUPS * P
assert C_END <= 2 * TILE

K_ID = 0
K_IOTA = K_ID + P
K_CINV = K_IOTA + P
K_TRIL = K_CINV + GROUPS * S
K_OH = K_TRIL + P
NDIST = 2 * P + P - 1
K_END = K_OH + NDIST

PLAN = (
    [("h1T", "V")] * 4 + [("q", "A")] * 2 + [("kv", "A")] + [("lg0", "V")] * 2 + [("lg1", "V")] * 4
    + [("pz", "V")] * 2 + [("gu", "A")] * 2 + [("gv", "A")] * 2 + [("pT0", "A")] * 2 + [("pT1", "A")] * 4
    + [("attn", "A")] * 4 + [("pool", "V")] * 2 + [("gmlp", "V")] * 2
    + ([("gate", "A")] * 2 + [("branch", "V")] * 2) * (2 * BR)
    + [("wo", "V")] * 4 + [("h2T", "V")] * 4 + [("qq", "A")] * 8 + [("score", "A")] * 8 + [("sel", "A")] * 2
)
NG = len(PLAN)
NBANK = 8
NGV = sum(who == "V" for _, who in PLAN)
NGA = NG - NGV
NCHAIN = 51
NSCAL = 8


def taken_before(group):
    return (sum(who == "V" for _, who in PLAN[:group]), sum(who == "A" for _, who in PLAN[:group]))


def first(name):
    return [n for n, _ in PLAN].index(name)


def program(nc, x_in, stream, consts_in, rel_in, fgain_in, out):
    ctx = ExitStack()
    with ctx:
        def sb(name, shape, dt=F32):
            return ctx.enter_context(nc.sbuf_tensor(name, shape, dt))

        def sem(name):
            return ctx.enter_context(nc.semaphore(name))

        ring = sb("ring", [P, RING, TILE])
        x = sb("x", [P, TT, D])
        hT = sb("hT", [P, KD, S])
        act = sb("act", [P, 2, S])
        coef = sb("coef", [P, 2, S])
        consts = sb("consts", [P, K_OH])
        stat = sb("stat", [P, 16])
        area = sb("area", [P, S * NK])
        used = [0]

        def part(*shape, dt=F32, at=None):
            n = int(np.prod(shape))
            a = used[0] if at is None else at
            used[0] = max(used[0], a + n)
            v = area[:, a:a + n]
            if dt != F32:
                v = v.bitcast(dt)
            if len(shape) == 1:
                return v
            names = [f"a{i}" for i in range(len(shape))]
            return v.rearrange(f"p ({' '.join(names)}) -> p {' '.join(names)}", **dict(zip(names[1:], shape[1:])))

        gates_t = area[:, :].rearrange("p (t e) -> p t e", t=S)
        par = part(2 * TILE)
        bias_a = sb("bias", [P, HEADS * 2 * P])
        bias = bias_a[:, :].rearrange("p (h s) -> p h s", h=HEADS)
        hn = part(TT, D)
        qT = part(QC, S)
        kT = part(S)
        v_tok = part(TT, P)
        lg0 = part(HEADS, P)
        lg1 = part(HEADS, 2 * P)
        pT0 = part(HEADS, P)
        pT1 = part(HEADS * 2, P)
        attnT = part(QC, S)
        zp = part(GROUPS, PAD + S)
        win = [part(GROUPS, PAD + S) for _ in POOL_WINDOWS]
        dT = part(GROUPS, S)
        poolT = part(GROUPS, S)
        uT = part(GROUPS, S)
        gv = part(TT, GROUPS * P)
        gmT = part(GROUPS, S)
        wsp = part(GROUPS, P)
        sig = part(2, 4, S)
        mergedT = part(KD, S)
        small = part(64)
        used_mix = used[0]
        used[0] = 2 * TILE
        qqT = part(PH, 2, S)
        row = part(TT, PH, 2, NK)
        val = part(TT, PH, 2, TOPK)
        idx = part(TT, PH, 2, TOPK, dt=U32)
        idf = part(TT, PH, 2, TOPK)
        cand = part(TT, PH, TOPK, TOPK)
        top = part(TT, PH, TOPK)
        ci = part(TT, PH, TOPK, dt=U32)
        ca = part(TT, PH, TOPK, dt=U32)
        cb = part(TT, PH, TOPK, dt=U32)
        caf = part(TT, PH, TOPK)
        cbf = part(TT, PH, TOPK)
        eq = part(PH, TOPK, TOPK)
        used[0] = max(used[0], used_mix)
        assert used[0] <= S * NK, used[0]
        sel = sb("sel", [P, 3, TT, P])
        selT = sb("selT", [P, 3, S])
        onehot1 = sb("onehot1", [P, 2, 2, NK])
        onehot2 = sb("onehot2", [P, 2, 2, NK])

        bank = [ctx.enter_context(nc.psum_tensor(f"bank{i}", [P, HALF_N], F32)) for i in range(NBANK)]
        acc = bank[0:4]
        bank_g = bank[4:6]
        bank_u = bank[6:8]
        act_row, coef_row = (b[:, :, :].rearrange("p s t -> p (s t)") for b in (act, coef))
        relx = act_row[0:BUCKETS + 1, 0:HEADS]
        relv = act_row[0:HEADS, HEADS:HEADS + NDIST]
        oh = coef_row[0:BUCKETS + 1, 0:NDIST]
        scratch = nc.dram_tensor("rel_scratch", (HEADS, P, NDIST), F32).ap()

        ident = consts[:, K_ID:K_ID + P]
        iota = consts[:, K_IOTA:K_IOTA + P]
        cinv = consts[:, K_CINV:K_CINV + GROUPS * S].rearrange("p (g t) -> p g t", g=GROUPS)
        tril = consts[:, K_TRIL:K_TRIL + P]

        loaded = [sem(f"loaded{i}") for i in range(RING)]
        tiles_used = sem("tiles_used")
        x_loaded = sem("x_loaded")
        consts_loaded = sem("consts_loaded")
        rel_loaded = sem("rel_loaded")
        rel_low = sem("rel_low")
        rel_product = sem("rel_product")
        rel_vector = sem("rel_vector")
        rel_written = sem("rel_written")
        bias_loaded = sem("bias_loaded")
        params_ready = sem("params_ready")
        wsp_ready = sem("wsp_ready")
        sumsq_ready = sem("sumsq_ready")
        root_ready = sem("root_ready")
        rstd_ready = sem("rstd_ready")
        hn_ready = sem("hn_ready")
        groups_done = sem("groups_done")
        taken_v = sem("taken_v")
        taken_a = sem("taken_a")
        chain = sem("chain")
        scal = sem("scal")
        max_ready = sem("max_ready")
        exp_ready = sem("exp_ready")
        probs_ready = sem("probs_ready")
        diff_ready = sem("diff_ready")
        vhat_ready = sem("vhat_ready")
        gm_ready = sem("gm_ready")
        merged_ready = sem("merged_ready")
        shifted_ready = sem("shifted_ready")
        gexp_ready = sem("gexp_ready")
        sel_ready = sem("sel_ready")
        onehots_ready = sem("onehots_ready")
        outer_done = sem("outer_done")
        table_ready = sem("table_ready")
        act_done = sem("act_done")
        coef_ready = sem("coef_ready")
        x_updated = sem("x_updated")
        fgain_loaded = sem("fgain_loaded")
        out_ready = sem("out_ready")
        out_written = sem("out_written")

        NPAIR = NK // 2
        NQUAD = S // 4

        block = ctx.enter_context(nc.Block())

        @block.sync
        def _(sp):
            sp.dma_start(x[:, :, :], x_in.rearrange("b (t p) d -> p (b t) d", p=P)).then_inc(x_loaded, 16)
            sp.dma_start(consts[:, :], consts_in[:, 0:K_OH]).then_inc(consts_loaded, 16)
            sp.dma_start(oh, consts_in[0:BUCKETS + 1, K_OH:K_END]).then_inc(rel_loaded, 16)
            sp.dma_start(relx[0:BUCKETS, :], rel_in).then_inc(rel_loaded, 16)
            for s in range(RING):
                sp.dma_start(ring[:, s, :], stream[s]).then_inc(loaded[s], 16)
            sp.wait_ge(rel_vector, 1)
            sp.dma_start(scratch, relv.unsqueeze(1).to_broadcast([HEADS, P, NDIST])).then_inc(rel_written, 16)
            sp.wait_ge(rel_written, 16)
            sp.dma_start(bias, bass.AP(scratch.tensor, P - 1, [[NDIST - 1, P], [P * NDIST, HEADS], [1, 2 * P]]))\
                .then_inc(bias_loaded, 16)
            with sp.Fori(1, DEPTH * NT // RING) as r:
                for s in range(RING):
                    sp.wait_ge(tiles_used, r * RING + (s - RING + 1))
                    sp.dma_start(ring[:, s, :], stream[bass.ds(r * RING + s, 1)].rearrange("a p c -> (a p) c"))\
                        .then_inc(loaded[s], 16)
            sp.wait_ge(x_updated, 2 * DEPTH)
            sp.dma_start(hT[:, 0:4, :].rearrange("p k t -> p (k t)"), fgain_in).then_inc(fgain_loaded, 16)
            sp.wait_ge(out_ready, TT)
            sp.dma_start(out.rearrange("b (t p) d -> p (b t) d", p=P), x[:, :, :]).then_inc(out_written, 16)
            sp.wait_ge(out_written, 16)

        @block.gpsimd
        def _(pool):
            pool.memset(relx[BUCKETS:BUCKETS + 1, :], NEG).then_inc(rel_low, 1)
            pool.wait_ge(rel_low, 1)
            pool.wait_ge(consts_loaded, 16)
            with pool.Fori(0, DEPTH) as l:
                pool.wait_ge(params_ready, l + 1)
                for g in range(GROUPS):
                    i = pool.tensor_tensor(wsp[:, g, :], par[:, C_WSP + g * P:C_WSP + (g + 1) * P], tril, ALU.mult)
                i.then_inc(wsp_ready, 1)

        @block.scalar
        def _(a):
            eps = stat[:, 15:16]

            def norm_sums(l, count, half):
                for t in range(TT):
                    i = a.activation(hn[:, t, :], x[:, t, :], ACT.Square, accum_out=stat[:, t:t + 1])
                    i.then_inc(scal, 1)
                a.wait_ge(scal, l * NSCAL + count + TT)
                a.activation(stat[:, 2:4], stat[:, 0:2], ACT.Sqrt, bias=eps, scale=1.0 / D).then_inc(root_ready, 1)
                a.wait_ge(rstd_ready, l * 3 + (1 if half == 0 else 3))
                for t in range(TT):
                    a.activation(hn[:, t, :], x[:, t, :], ACT.Copy, scale=stat[:, 4 + t:5 + t]).then_inc(hn_ready, 1)

            a.wait_ge(x_loaded, 16)
            a.wait_ge(chain, 1)
            with a.Fori(0, DEPTH) as l:
                g = [0, 0]

                def group(name):
                    while PLAN[g[0]][1] != "A":
                        g[0] += 1
                    assert PLAN[g[0]][0] == name, (PLAN[g[0]], name)
                    a.wait_ge(groups_done, l * NG + (g[0] + 1))
                    g[0] += 1
                    return bank[(g[0] - 1) % NBANK]

                a.wait_ge(x_updated, l * 2)
                for n in range(2):
                    a.wait_ge(loaded[n], l * (16 * NT // RING) + 16)
                    a.activation(par[:, n * TILE:(n + 1) * TILE], ring[:, n, :], ACT.Copy).then_inc(scal, 1)
                a.wait_ge(scal, l * NSCAL + 2)
                a.sem_inc(params_ready, 1)
                norm_sums(l, 2, 0)
                for n in range(2):
                    b = group("q")
                    a.activation(qT[:, 2 * n:2 * n + 2, :], b[:, :].rearrange("p (c t) -> p c t", c=2), ACT.Copy)\
                        .then_inc(taken_a, 1)
                b = group("kv")
                a.activation(kT, b[:, 0:S], ACT.Copy)
                a.activation(v_tok, b[:, S:].rearrange("p (t c) -> p t c", t=TT), ACT.Copy).then_inc(taken_a, 1)
                for n in range(2):
                    b = group("gu")
                    a.activation(uT[:, 2 * n:2 * n + 2, :], b[:, :].rearrange("p (c t) -> p c t", c=2),
                                 ACT.Gelu_apprx_tanh).then_inc(taken_a, 1)
                for t in range(TT):
                    b = group("gv")
                    a.activation(gv[:, t, :], b[:, :], ACT.Gelu_apprx_tanh).then_inc(taken_a, 1)
                a.wait_ge(taken_a, l * NGA + 7)
                for t in range(TT):
                    a.activation(hn[:, t, 0:GROUPS * P], gv[:, t, :], ACT.Square, accum_out=stat[:, 6 + t:7 + t])\
                        .then_inc(scal, 1)
                a.wait_ge(scal, l * NSCAL + 6)
                a.activation(stat[:, 8:10], stat[:, 6:8], ACT.Sqrt, bias=eps, scale=1.0 / (GROUPS * P))\
                    .then_inc(root_ready, 1)
                for blk, lg in ((0, lg0), (1, lg1)):
                    a.wait_ge(max_ready, l * 2 + (blk + 1))
                    for h in range(HEADS):
                        a.activation(lg[:, h, :], lg[:, h, :], ACT.Exp, bias=small[:, blk * 32 + h:blk * 32 + h + 1],
                                     accum_out=small[:, blk * 32 + 16 + h:blk * 32 + 17 + h])
                    a.activation(small[:, blk * 32 + 24:blk * 32 + 32], small[:, blk * 32 + 8:blk * 32 + 16], ACT.Exp)\
                        .then_inc(exp_ready, 1)
                for n in range(2):
                    b = group("pT0")
                    a.activation(pT0[:, 4 * n:4 * n + 4, :], b[:, :].rearrange("p (c t) -> p c t", c=4), ACT.Copy)\
                        .then_inc(taken_a, 1)
                for n in range(4):
                    b = group("pT1")
                    a.activation(pT1[:, 4 * n:4 * n + 4, :], b[:, :].rearrange("p (c t) -> p c t", c=4), ACT.Copy)\
                        .then_inc(taken_a, 1)
                for c in range(QC):
                    b = group("attn")
                    a.activation(attnT[0:HD, c, :], b[0:HD, 0:S], ACT.Copy)
                    a.activation(attnT[HD:P, c, :], b[HD:P, S:], ACT.Copy).then_inc(taken_a, 1)
                for hf in range(2):
                    for br in range(BR):
                        if 3 * hf + br >= 2:
                            a.wait_ge(taken_v, l * NGV + taken_before(first("gate") + 4 * (3 * hf + br - 1))[0])
                        for n in range(2):
                            b = group("gate")
                            for c in range(2):
                                col = C_BGATE + br * KD + hf * 4 + 2 * n + c
                                i = a.activation(sig[:, (3 * hf + br) % 2, 2 * n + c, :], b[:, c * S:(c + 1) * S],
                                                 ACT.Sigmoid, bias=par[:, col:col + 1])
                            i.then_inc(taken_a, 1)
                a.wait_ge(x_updated, l * 2 + 1)
                norm_sums(l, 6, 1)
                for h in range(PH):
                    b = group("qq")
                    a.activation(qqT[:, h], b[:, :].rearrange("p (c t) -> p c t", c=2), ACT.Copy).then_inc(taken_a, 1)
                for n in range(8):
                    b = group("score")
                    a.activation(row[:, n // 4, 2 * (n % 4):2 * (n % 4) + 2].rearrange("p h c k -> p (h c k)"),
                                 b[:, :], ACT.Copy).then_inc(taken_a, 1)
                a.wait_ge(shifted_ready, l + 1)
                a.activation(sel[:, 2], sel[:, 2], ACT.Exp).then_inc(gexp_ready, 1)
                for t in range(TT):
                    b = group("sel")
                    a.activation(selT[:, :, t * P:(t + 1) * P], b[:, 0:3 * P].rearrange("p (c t) -> p c t", c=3),
                                 ACT.Copy).then_inc(taken_a, 1)
                with a.Fori(0, NQUAD) as j:
                    for s in range(2):
                        a.wait_ge(outer_done, l * 2 * NQUAD + j * 2 + (s + 1))
                        a.activation(gates_t[:, bass.ds(j * 4 + 2 * s, 2), :],
                                     bank_g[s][:, 0:2 * NK].rearrange("p (t e) -> p t e", t=2), ACT.Copy)\
                            .then_inc(table_ready, 1)

                def gelu(b, s, reuse):
                    a.wait_ge(tiles_used, l * NT + b * 2 + (T_UV if reuse or s else T_UV + 1))
                    if reuse:
                        a.wait_ge(coef_ready, l * NK + b - 1)
                    a.activation(act[:, s, :], bank_u[s][:, 0:S], ACT.Gelu_apprx_tanh).then_inc(act_done, 1)

                gelu(0, 0, False)
                gelu(1, 1, False)
                with a.Fori(1, NPAIR) as j:
                    gelu(j * 2, 0, True)
                    gelu(j * 2 + 1, 1, True)
            a.wait_ge(x_updated, 2 * DEPTH)
            for t in range(TT):
                a.activation(hn[:, t, :], x[:, t, :], ACT.Square, accum_out=stat[:, t:t + 1]).then_inc(scal, 1)
            a.wait_ge(scal, NSCAL * DEPTH + TT)
            a.activation(stat[:, 2:4], stat[:, 0:2], ACT.Sqrt, bias=eps, scale=1.0 / D).then_inc(root_ready, 1)
            a.wait_ge(rstd_ready, 3 * DEPTH + 1)
            for t in range(TT):
                a.activation(hn[:, t, :], x[:, t, :], ACT.Copy, scale=stat[:, 4 + t:5 + t]).then_inc(hn_ready, 1)

        @block.vector
        def _(v):
            v.memset(stat[:, 15:16], EPS).then_inc(chain, 1)
            v.wait_ge(rel_product, 1)
            v.tensor_copy(relv, bank[0][0:HEADS, 0:NDIST]).then_inc(rel_vector, 1)

            with v.Fori(0, DEPTH) as l:
                links = [1]

                def link(ins):
                    links[0] += 1
                    ins.then_inc(chain, 1)
                    v.wait_ge(chain, l * NCHAIN + links[0])

                g = [0]

                def group(name):
                    while PLAN[g[0]][1] != "V":
                        g[0] += 1
                    assert PLAN[g[0]][0] == name, (PLAN[g[0]], name)
                    v.wait_ge(groups_done, l * NG + (g[0] + 1))
                    g[0] += 1
                    return bank[(g[0] - 1) % NBANK]

                def transposed(name, col):
                    for t in range(TT):
                        for n in range(2):
                            b = group(name)
                            v.tensor_tensor(
                                hT[:, 4 * n:4 * n + 4, t * P:(t + 1) * P], b[:, :].rearrange("p (k t) -> p k t", k=4),
                                par[:, col + 4 * n:col + 4 * n + 4].unsqueeze(2).to_broadcast([P, 4, P]), ALU.mult,
                            ).then_inc(taken_v, 1)

                def rstd(n, at, to):
                    v.wait_ge(root_ready, l * 3 + n)
                    v.reciprocal(stat[:, to:to + 2], stat[:, at:at + 2]).then_inc(rstd_ready, 1)

                rstd(1, 2, 4)
                v.wait_ge(params_ready, l + 1)
                transposed("h1T", C_AGAIN)
                v.wait_ge(bias_loaded, 16)
                for blk, lg, per in ((0, lg0, 4), (1, lg1, 2)):
                    for n in range(HEADS // per):
                        b = group(f"lg{blk}")
                        i = v.scalar_tensor_tensor(
                            lg[:, per * n:per * n + per, :], b[:, :].rearrange("p (h s) -> p h s", h=per), HD ** -0.5,
                            bias[:, per * n:per * n + per, (1 - blk) * P:], ALU.mult, ALU.add)
                        i.then_inc(taken_v, 1)
                    v.wait_ge(taken_v, l * NGV + (6 if blk == 0 else 10))
                    o = blk * 32
                    link(v.tensor_reduce(small[:, o:o + 8], lg, AX.X, ALU.max))
                    link(v.tensor_tensor(small[:, o:o + 8], small[:, o:o + 8], par[:, C_SINK:C_SINK + 8], ALU.max))
                    link(v.tensor_scalar(small[:, o:o + 8], small[:, o:o + 8], -1.0, None, ALU.mult))
                    v.tensor_tensor(small[:, o + 8:o + 16], small[:, o:o + 8], par[:, C_SINK:C_SINK + 8], ALU.add)\
                        .then_inc(max_ready, 1)
                link(v.memset(zp[:, :, 0:PAD], 0.0))
                for n in range(2):
                    b = group("pz")
                    v.tensor_copy(zp[:, 2 * n:2 * n + 2, PAD:], b[:, :].rearrange("p (c t) -> p c t", c=2))\
                        .then_inc(taken_v, 1)
                v.wait_ge(taken_v, l * NGV + 12)
                src = zp
                for n, w in enumerate(POOL_WINDOWS):
                    link(v.tensor_tensor(win[n][:, n:, w - 1:], src[:, n:, w - 1:],
                                         src[:, n:, w - 1 - w // 2:PAD + S - w // 2], ALU.add))
                    src = win[n]
                for n in range(GROUPS):
                    i = v.tensor_tensor(dT[:, n, :], win[n][:, n, PAD:], cinv[:, n, :], ALU.mult)
                link(i)
                v.tensor_tensor(dT, dT, zp[:, :, PAD:], ALU.subtract).then_inc(diff_ready, 1)
                rstd(2, 8, 10)
                v.wait_ge(rstd_ready, l * 3 + 2)
                for t in range(TT):
                    i = v.tensor_scalar(gv[:, t, :], gv[:, t, :], stat[:, 10 + t:11 + t], None, ALU.mult)
                i.then_inc(vhat_ready, 1)
                for blk, lg in ((0, lg0), (1, lg1)):
                    o = blk * 32
                    v.wait_ge(exp_ready, l * 2 + (blk + 1))
                    link(v.tensor_tensor(small[:, o + 16:o + 24], small[:, o + 16:o + 24], small[:, o + 24:o + 32], ALU.add))
                    link(v.reciprocal(small[:, o + 16:o + 24], small[:, o + 16:o + 24]))
                    v.tensor_tensor(lg, lg, small[:, o + 16:o + 24].unsqueeze(2).to_broadcast([P, HEADS, (blk + 1) * P]),
                                    ALU.mult).then_inc(probs_ready, 1)
                for n in range(2):
                    b = group("pool")
                    v.tensor_tensor(
                        poolT[:, 2 * n:2 * n + 2, :], b[:, :].rearrange("p (c t) -> p c t", c=2),
                        par[:, C_PSCALE + 2 * n:C_PSCALE + 2 * n + 2].unsqueeze(2).to_broadcast([P, 2, S]), ALU.mult,
                    ).then_inc(taken_v, 1)
                bsp = par[:, C_BSP:C_BSP + GROUPS * P].rearrange("p (g t) -> p g t", g=GROUPS)
                for n in range(2):
                    b = group("gmlp")
                    for c in range(2):
                        i = v.scalar_tensor_tensor(
                            gmT[:, 2 * n + c, :].rearrange("p (c t) -> p c t", c=2),
                            b[:, c * S:(c + 1) * S].rearrange("p (c t) -> p c t", c=2),
                            par[:, C_VGAIN + 2 * n + c:C_VGAIN + 2 * n + c + 1],
                            bsp[:, 2 * n + c, :].unsqueeze(1).to_broadcast([P, 2, P]), ALU.mult, ALU.add)
                    i.then_inc(taken_v, 1)
                v.wait_ge(taken_v, l * NGV + 16)
                v.wait_ge(taken_a, l * NGA + 5)
                v.tensor_tensor(gmT, gmT, uT, ALU.mult).then_inc(gm_ready, 1)
                v.wait_ge(gm_ready, l + 1)
                for hf in range(2):
                    for br in range(BR):
                        for n in range(2):
                            b = group("branch")
                            y = b[:, :].rearrange("p (c t) -> p c t", c=2)
                            m = mergedT[:, 4 * hf + 2 * n:4 * hf + 2 * n + 2, :]
                            s = sig[:, (3 * hf + br) % 2, 2 * n:2 * n + 2, :]
                            v.wait_ge(taken_a, l * NGA + taken_before(g[0])[1])
                            if br == 0:
                                v.tensor_tensor(m, s, y, ALU.mult).then_inc(taken_v, 1)
                            else:
                                tmp = zp[:, 2 * n:2 * n + 2, 0:S]
                                i = v.tensor_tensor(tmp, s, y, ALU.mult)
                                i.then_inc(taken_v, 1)
                                v.wait_ge(taken_v, l * NGV + taken_before(g[0])[0])
                                link(v.tensor_tensor(m, m, tmp, ALU.add))
                v.sem_inc(merged_ready, 1)
                for hf in range(2):
                    for t in range(TT):
                        b = group("wo")
                        xs = x[:, t, hf * HALF_N:(hf + 1) * HALF_N]
                        v.tensor_tensor(xs, xs, b[:, :], ALU.add).then_inc(taken_v, 1)
                v.wait_ge(taken_v, l * NGV + taken_before(first("h2T"))[0])
                v.sem_inc(x_updated, 1)
                rstd(3, 2, 4)
                transposed("h2T", C_FGAIN)

                def then_search(ins):
                    links[0] += 1
                    ins.then_inc(chain, 1)
                    v.wait_ge(chain, l * NCHAIN + links[0])
                    v.memset(stat[:, 14:15], 0.0)

                v.wait_ge(taken_a, l * NGA + NGA - 2)
                v.memset(stat[:, 14:15], 0.0)
                rows = [(t, h, c) for t in range(TT) for h in range(PH) for c in range(2)]
                for k in range(2):
                    for t, h, c in rows:
                        i = v.max(val[:, t, h, c, 8 * k:8 * k + 8], row[:, t, h, c, :])
                    then_search(i)
                    for t, h, c in rows:
                        i = v.max_index(idx[:, t, h, c, 8 * k:8 * k + 8], val[:, t, h, c, 8 * k:8 * k + 8], row[:, t, h, c, :])
                    then_search(i)
                    if k == 0:
                        for t, h, c in rows:
                            i = v.match_replace(row[:, t, h, c, :], val[:, t, h, c, 0:8], row[:, t, h, c, :], LOW)
                        then_search(i)
                v.tensor_copy(idf.rearrange("p a b c d -> p (a b c d)"), idx.rearrange("p a b c d -> p (a b c d)"))
                for t in range(TT):
                    i = v.tensor_tensor(cand[:, t], val[:, t, :, 0, :].unsqueeze(3).to_broadcast([P, PH, TOPK, TOPK]),
                                        val[:, t, :, 1, :].unsqueeze(2).to_broadcast([P, PH, TOPK, TOPK]), ALU.add)
                then_search(i)
                pairs = [(t, h) for t in range(TT) for h in range(PH)]
                for k in range(2):
                    ks = slice(8 * k, 8 * k + 8)
                    flat = [cand[:, t, h].rearrange("p a b -> p (a b)") for t, h in pairs]
                    for (t, h), f in zip(pairs, flat):
                        i = v.max(top[:, t, h, ks], f)
                    then_search(i)
                    for (t, h), f in zip(pairs, flat):
                        i = v.max_index(ci[:, t, h, ks], top[:, t, h, ks], f)
                    then_search(i)
                    if k == 0:
                        for (t, h), f in zip(pairs, flat):
                            i = v.match_replace(f, top[:, t, h, ks], f, LOW)
                        then_search(i)
                gate = sel[:, 2].rearrange("p t (h j) -> p t h j", h=PH)
                for t in range(TT):
                    i = v.tensor_tensor(gate[:, t], top[:, t], top[:, t, :, 0:1].to_broadcast([P, PH, TOPK]), ALU.subtract)
                i.then_inc(shifted_ready, 1)
                v.tensor_scalar(ca.rearrange("p t h j -> p (t h j)"), ci.rearrange("p t h j -> p (t h j)"), 4, None,
                                ALU.logical_shift_right)
                link(v.tensor_scalar(cb.rearrange("p t h j -> p (t h j)"), ci.rearrange("p t h j -> p (t h j)"), 15, None,
                                     ALU.bitwise_and))
                v.tensor_copy(caf, ca)
                link(v.tensor_copy(cbf, cb))
                for c, rank in ((0, caf), (1, cbf)):
                    for t in range(TT):
                        link(v.tensor_tensor(eq, rank[:, t].unsqueeze(3).to_broadcast([P, PH, TOPK, TOPK]),
                                             iota[:, 0:TOPK].unsqueeze(1).unsqueeze(1).to_broadcast([P, PH, TOPK, TOPK]),
                                             ALU.is_equal))
                        link(v.tensor_tensor(eq, eq, idf[:, t, :, c, :].unsqueeze(2).to_broadcast([P, PH, TOPK, TOPK]),
                                             ALU.mult))
                        link(v.tensor_reduce(sel[:, c, t].rearrange("p (h j) -> p h j", h=PH), eq, AX.X, ALU.add))
                v.wait_ge(gexp_ready, l + 1)
                gs = small[:, 0:16].rearrange("p (t h) -> p t h", t=TT)
                link(v.tensor_reduce(gs, gate, AX.X, ALU.add))
                link(v.reciprocal(gs, gs))
                for t in range(TT):
                    i = v.tensor_tensor(gate[:, t], gate[:, t], gs[:, t].unsqueeze(2).to_broadcast([P, PH, TOPK]), ALU.mult)
                i.then_inc(sel_ready, 1)
                v.wait_ge(taken_a, l * NGA + NGA)
                def onehots(j, s, reuse):
                    if reuse:
                        v.wait_ge(outer_done, l * 2 * NQUAD + j * 2 + s - 1)
                    for u in range(2):
                        t = j * 4 + (2 * s + u)
                        key1, key2, weight = (selT[:, c, bass.ds(t, 1)] for c in range(3))
                        v.tensor_scalar(onehot1[:, s, u, :], iota, key1, None, ALU.is_equal)
                        i = v.tensor_scalar(onehot2[:, s, u, :], iota, key2, weight, ALU.is_equal, ALU.mult)
                    i.then_inc(onehots_ready, 1)

                onehots(0, 0, False)
                onehots(0, 1, False)
                with v.Fori(1, NQUAD) as j:
                    onehots(j, 0, True)
                    onehots(j, 1, True)
                v.wait_ge(table_ready, l * 2 * NQUAD + 2 * NQUAD)

                def gated(b, s, reuse):
                    v.wait_ge(act_done, l * NK + b + 1)
                    if reuse:
                        v.wait_ge(tiles_used, l * NT + b * 2 + (T_UV - 1))
                    v.tensor_tensor(coef[:, s, :].unsqueeze(2), act[:, s, :].unsqueeze(2), gates_t[:, :, bass.ds(b, 1)], ALU.mult)\
                        .then_inc(coef_ready, 1)

                gated(0, 0, False)
                gated(1, 1, False)
                with v.Fori(1, NPAIR) as j:
                    gated(j * 2, 0, True)
                    gated(j * 2 + 1, 1, True)
                v.wait_ge(tiles_used, l * NT + NT)
                for t in range(TT):
                    for hf in range(2):
                        xs = x[:, t, hf * HALF_N:(hf + 1) * HALF_N]
                        i = v.tensor_tensor(xs, xs, acc[2 * t + hf][:, :], ALU.add)
                i.then_inc(x_updated, 1)
                v.wait_ge(x_updated, l * 2 + 2)
                assert links[0] == NCHAIN + 1, links[0]
            v.wait_ge(root_ready, 3 * DEPTH + 1)
            v.reciprocal(stat[:, 4:6], stat[:, 2:4]).then_inc(rstd_ready, 1)
            v.wait_ge(fgain_loaded, 16)
            for t in range(TT):
                v.wait_ge(hn_ready, 2 * TT * DEPTH + t + 1)
                v.tensor_tensor(x[:, t, :], hn[:, t, :], hT[:, 0:4, :].rearrange("p k t -> p (k t)"), ALU.mult)\
                    .then_inc(out_ready, 1)

        @block.tensor
        def _(pe):
            pe.wait_ge(consts_loaded, 16)
            pe.wait_ge(rel_loaded, 32)
            pe.wait_ge(rel_low, 1)
            pe.matmul(bank[0][0:HEADS, 0:NDIST], relx, oh, start=True, stop=True).then_inc(rel_product, 1)
            pe.wait_ge(rel_vector, 1)

            with pe.Fori(0, DEPTH) as l:
                g = [0]

                def group(name):
                    assert PLAN[g[0]][0] == name, (PLAN[g[0]], name)
                    if g[0] >= NBANK:
                        prev = g[0] - NBANK
                        tv, ta = taken_before(prev + 1)
                        if PLAN[prev][1] == "V":
                            pe.wait_ge(taken_v, l * NGV + tv)
                        else:
                            pe.wait_ge(taken_a, l * NGA + ta)
                    g[0] += 1
                    return bank[(g[0] - 1) % NBANK]

                def tile(n):
                    pe.wait_ge(loaded[n % RING], l * (16 * NT // RING) + 16 * (n // RING + 1))
                    return ring[:, n % RING, :]

                def columns(n, o):
                    w = tile(n).rearrange("p (k c) -> p k c", k=KD)
                    for k in range(KD):
                        i = pe.matmul(o, w[:, k, :], hT[:, k, :], start=k == 0, stop=k == KD - 1)
                        if k == 0:
                            i.then_inc(tiles_used, 1)
                    return i

                def transpose_rows(name):
                    for t in range(TT):
                        for n in range(2):
                            b = group(name)
                            for k in range(4):
                                i = pe.transpose(b[:, k * P:(k + 1) * P], hn[:, t, (4 * n + k) * P:(4 * n + k + 1) * P], ident)
                            i.then_inc(groups_done, 1)

                pe.wait_ge(params_ready, l + 1)
                pe.sem_inc(tiles_used, 1)
                pe.wait_ge(hn_ready, l * 2 * TT + TT)
                transpose_rows("h1T")
                pe.wait_ge(taken_v, l * NGV + 4)
                for n in range(QC // 2):
                    b = group("q")
                    for c in range(2):
                        i = columns(T_Q + 2 * n + c, b[:, c * S:(c + 1) * S])
                    i.then_inc(groups_done, 1)
                b = group("kv")
                columns(T_K, b[:, 0:S])
                w = tile(T_V).rearrange("p (k c) -> p k c", k=KD)
                for t in range(TT):
                    for k in range(KD):
                        i = pe.matmul(b[:, S + t * P:S + (t + 1) * P], hT[:, k, t * P:(t + 1) * P], w[:, k, :],
                                      start=k == 0, stop=k == KD - 1)
                        if t == 0 and k == 0:
                            i.then_inc(tiles_used, 1)
                i.then_inc(groups_done, 1)
                pe.wait_ge(taken_a, l * NGA + 3)
                for blk, per in ((0, 4), (1, 2)):
                    width = (blk + 1) * P
                    for n in range(HEADS // per):
                        b = group(f"lg{blk}")
                        for u in range(per):
                            h = per * n + u
                            rows = slice(0, HD) if h < 4 else slice(HD, P)
                            i = pe.matmul(b[:, u * width:(u + 1) * width], qT[rows, h % 4, blk * P:(blk + 1) * P],
                                          kT[rows, 0:width], start=True, stop=True)
                        i.then_inc(groups_done, 1)
                for name, t0 in (("pz", T_PZ), ("gu", T_GU)):
                    for n in range(GROUPS // 2):
                        b = group(name)
                        for c in range(2):
                            i = columns(t0 + 2 * n + c, b[:, c * S:(c + 1) * S])
                        i.then_inc(groups_done, 1)
                b = [group("gv") for _ in range(TT)]
                for c in range(2):
                    for kh in range(2):
                        w = tile(T_GV + 2 * c + kh).rearrange("p (k c) -> p k c", k=4)
                        for t in range(TT):
                            for k in range(4):
                                i = pe.matmul(b[t][:, c * S:(c + 1) * S], hT[:, 4 * kh + k, t * P:(t + 1) * P], w[:, k, :],
                                              start=kh == 0 and k == 0, stop=kh == 1 and k == 3)
                                if t == 0 and k == 0:
                                    i.then_inc(tiles_used, 1)
                            if c == 1 and kh == 1:
                                i.then_inc(groups_done, 1)
                pe.wait_ge(probs_ready, l * 2 + 1)
                for n in range(2):
                    b = group("pT0")
                    for u in range(4):
                        i = pe.transpose(b[:, u * P:(u + 1) * P], lg0[:, 4 * n + u, :], ident)
                    i.then_inc(groups_done, 1)
                pe.wait_ge(probs_ready, l * 2 + 2)
                for n in range(4):
                    b = group("pT1")
                    for u in range(4):
                        i = pe.transpose(b[:, u * P:(u + 1) * P], lg1[:, 2 * n + u // 2, (u % 2) * P:(u % 2 + 1) * P], ident)
                    i.then_inc(groups_done, 1)
                pe.wait_ge(taken_a, l * NGA + taken_before(first("attn"))[1])
                for c in range(QC):
                    b = group("attn")
                    for u in range(2):
                        h = c + 4 * u
                        pe.matmul(b[:, u * S:u * S + P], v_tok[:, 0, :], pT0[:, h, :], start=True, stop=True)
                        for sblk in range(2):
                            i = pe.matmul(b[:, u * S + P:(u + 1) * S], v_tok[:, sblk, :], pT1[:, 2 * h + sblk, :],
                                          start=sblk == 0, stop=sblk == 1)
                    i.then_inc(groups_done, 1)
                pe.wait_ge(diff_ready, l + 1)
                for n in range(2):
                    b = group("pool")
                    for c in range(2):
                        gg = 2 * n + c
                        i = pe.matmul(b[:, c * S:(c + 1) * S], par[:, C_WPOOL + gg * P:C_WPOOL + (gg + 1) * P], dT[:, gg, :],
                                      start=True, stop=True)
                    i.then_inc(groups_done, 1)
                pe.wait_ge(vhat_ready, l + 1)
                pe.wait_ge(wsp_ready, l + 1)
                for n in range(2):
                    b = group("gmlp")
                    for c in range(2):
                        gg = 2 * n + c
                        for t in range(TT):
                            i = pe.matmul(b[:, c * S + t * P:c * S + (t + 1) * P], gv[:, t, gg * P:(gg + 1) * P],
                                          wsp[:, gg, :], start=True, stop=True)
                    i.then_inc(groups_done, 1)
                pe.wait_ge(taken_a, l * NGA + taken_before(first("gate"))[1])
                for hf in range(2):
                    for br, mixed in enumerate((attnT, poolT, gmT)):
                        t0 = T_MIX + hf * MIX_HALF + br * 6
                        for n in range(2):
                            b = group("gate")
                            for c in range(2):
                                i = columns(t0 + 2 * n + c, b[:, c * S:(c + 1) * S])
                            i.then_inc(groups_done, 1)
                        if hf == 0 and br == 1:
                            pe.wait_ge(taken_v, l * NGV + taken_before(first("gmlp"))[0])
                        if hf == 0 and br == 2:
                            pe.wait_ge(gm_ready, l + 1)
                        for n in range(2):
                            b = group("branch")
                            w = tile(t0 + 4 + n).rearrange("p (k c) -> p k c", k=4)
                            for c in range(2):
                                for k in range(4):
                                    i = pe.matmul(b[:, c * S:(c + 1) * S], w[:, k, c * P:(c + 1) * P], mixed[:, k, :],
                                                  start=k == 0, stop=k == 3)
                                    if c == 0 and k == 0:
                                        i.then_inc(tiles_used, 1)
                            i.then_inc(groups_done, 1)
                pe.wait_ge(merged_ready, l + 1)
                for hf in range(2):
                    b = [group("wo") for _ in range(TT)]
                    for kq in range(4):
                        w = tile(T_WO + 4 * hf + kq).rearrange("p (k c) -> p k c", k=2)
                        for t in range(TT):
                            for k in range(2):
                                i = pe.matmul(b[t][:, :], mergedT[:, 2 * kq + k, t * P:(t + 1) * P], w[:, k, :],
                                              start=kq == 0 and k == 0, stop=kq == 3 and k == 1)
                                if t == 0 and k == 0:
                                    i.then_inc(tiles_used, 1)
                            if kq == 3:
                                i.then_inc(groups_done, 1)
                pe.wait_ge(hn_ready, l * 2 * TT + 2 * TT)
                transpose_rows("h2T")
                pe.wait_ge(taken_v, l * NGV + NGV)
                for h in range(PH):
                    b = group("qq")
                    for c in range(2):
                        i = columns(T_WQ + 2 * h + c, b[:, c * S:(c + 1) * S])
                    i.then_inc(groups_done, 1)
                pe.wait_ge(taken_a, l * NGA + taken_before(first("score"))[1])
                for n in range(8):
                    b = group("score")
                    for u in range(2):
                        for c in range(2):
                            h, t = 2 * (n % 4) + u, n // 4
                            i = pe.matmul(b[:, (2 * u + c) * NK:(2 * u + c + 1) * NK], qqT[:, h, c, t * P:(t + 1) * P],
                                          par[:, C_SK + c * NK:C_SK + (c + 1) * NK], start=True, stop=True)
                    i.then_inc(groups_done, 1)
                pe.wait_ge(sel_ready, l + 1)
                for t in range(TT):
                    b = group("sel")
                    for c in range(3):
                        i = pe.transpose(b[:, c * P:(c + 1) * P], sel[:, c, t, :], ident)
                    i.then_inc(groups_done, 1)
                assert g[0] == NG

                def outer(j, s, reuse):
                    pe.wait_ge(onehots_ready, l * 2 * NQUAD + j * 2 + s + 1)
                    if reuse:
                        pe.wait_ge(table_ready, l * 2 * NQUAD + j * 2 + s - 1)
                    for u in range(2):
                        i = pe.matmul(bank_g[s][:, u * NK:(u + 1) * NK], onehot1[:, s, u, :], onehot2[:, s, u, :],
                                      start=True, stop=True)
                    i.then_inc(outer_done, 1)

                pe.wait_ge(taken_a, l * NGA + NGA)
                outer(0, 0, False)
                outer(0, 1, False)
                with pe.Fori(1, NQUAD) as j:
                    outer(j, 0, True)
                    outer(j, 1, True)

                def slot(n, rounds):
                    pe.wait_ge(loaded[n % RING], l * (16 * NT // RING) + rounds * 16)
                    return ring[:, n % RING, :]

                def u_product(b, s, n, rounds, reuse):
                    w = slot(n, rounds).rearrange("p (k c) -> p k c", k=KD)
                    if reuse:
                        pe.wait_ge(act_done, l * NK + b - 1)
                    for k in range(KD):
                        i = pe.matmul(bank_u[s][:, 0:S], w[:, k, :], hT[:, k, :], start=k == 0, stop=k == KD - 1)
                        if k == 0 and n == T_UV:
                            i.then_inc(tiles_used, 1)
                    i.then_inc(tiles_used, 1)

                def v_product(b, s, n, rounds, begin, end):
                    w = slot(n, rounds)
                    pe.wait_ge(coef_ready, l * NK + b + 1)
                    for t in range(TT):
                        for hf in range(2):
                            i = pe.matmul(acc[2 * t + hf][:, :], coef[:, s, t * P:(t + 1) * P],
                                          w[:, hf * HALF_N:(hf + 1) * HALF_N], start=begin, stop=end,
                                          skip_group_check=True)
                    i.then_inc(tiles_used, 1)

                r0 = T_UV // RING
                u_product(0, 0, T_UV, r0 + 1, False)
                u_product(1, 1, T_UV + 1, r0 + 1, False)
                v_product(0, 0, T_UV + 2, r0 + 1, True, False)
                u_product(2, 0, T_UV + 3, r0 + 1, True)
                v_product(1, 1, T_UV + 4, r0 + 2, False, False)
                with pe.Fori(1, NPAIR - 1) as j:
                    u_product(j * 2 + 1, 1, 1, j + (r0 + 1), True)
                    v_product(j * 2, 0, 2, j + (r0 + 1), False, False)
                    u_product(j * 2 + 2, 0, 3, j + (r0 + 1), True)
                    v_product(j * 2 + 1, 1, 0, j + (r0 + 2), False, False)
                u_product(NK - 1, 1, 1, NT // RING, True)
                v_product(NK - 2, 0, 2, NT // RING, False, False)
                v_product(NK - 1, 1, 3, NT // RING, False, True)


def shape_constants():
    c = np.zeros((P, K_END), np.float32)
    c[:, K_ID:K_ID + P] = np.eye(P)
    c[:, K_IOTA:K_IOTA + P] = np.arange(P)
    for g, w in enumerate(POOL_WINDOWS):
        c[:, K_CINV + g * S:K_CINV + (g + 1) * S] = 1.0 / np.minimum(np.arange(1, S + 1), w)
    c[:, K_TRIL:K_TRIL + P] = np.triu(np.ones((P, P)))
    exact = BUCKETS // 2
    for j in range(NDIST):
        dist = 2 * P - 1 - j
        if dist >= WINDOW or dist < 0:
            b = BUCKETS
        elif dist < exact:
            b = dist
        else:
            b = min(BUCKETS - 1, exact + int(np.log(dist / exact) / np.log(MAX_DIST / exact) * (BUCKETS - exact)))
        c[b, K_OH + j] = 1.0
    return c


def lay_out(inp):
    w_in = inp["w_in"]
    n_q, n_kv = HEADS * HD, 2 * HD
    order = np.concatenate([np.r_[c * HD:(c + 1) * HD, (c + 4) * HD:(c + 5) * HD] for c in range(QC)])
    out = np.zeros((DEPTH, NT, P, TILE), np.float32)

    def cols(w, c0, n):
        return w[:, c0:c0 + n * P].reshape(KD, P, n, P).transpose(2, 1, 0, 3).reshape(n, P, TILE)

    for l in range(DEPTH):
        o, w = out[l], w_in[l]
        par = np.zeros((P, 2 * TILE), np.float32)
        par[:, C_SK:C_SK + NK] = inp["peer_sub_keys1"][l].T
        par[:, C_SK + NK:C_SK + 2 * NK] = inp["peer_sub_keys2"][l].T
        par[:, C_WPOOL:C_WPOOL + GROUPS * P] = inp["w_pool"][l].transpose(1, 0, 2).reshape(P, -1)
        par[:, C_WSP:C_WSP + GROUPS * P] = inp["w_spatial"][l].transpose(2, 0, 1).reshape(P, -1)
        for c, name, k in ((C_AGAIN, "attn_norm_gain", KD), (C_FGAIN, "ffn_norm_gain", KD), (C_BGATE, "b_gate", BR * KD),
                           (C_PSCALE, "pool_scale", GROUPS), (C_VGAIN, "gmlp_v_gain", GROUPS)):
            par[:, c:c + k] = inp[name][l].reshape(k, P).T
        par[:, C_SINK:C_SINK + HEADS] = inp["attn_sinks"][l][None]
        par[:, C_BSP:C_BSP + GROUPS * P] = inp["b_spatial"][l].reshape(1, -1)
        o[T_PARAM:T_Q] = par.reshape(P, 2, TILE).transpose(1, 0, 2)
        o[T_Q:T_K] = cols(w[:, order], 0, QC)
        o[T_K:T_PZ] = cols(w, n_q, 2)
        c0 = n_q + 2 * n_kv
        o[T_PZ:T_GU] = cols(w, c0, GROUPS)
        o[T_GU:T_GV] = cols(w, c0 + GROUPS * P, GROUPS)
        c0 += 2 * GROUPS * P
        o[T_GV:T_MIX] = w[:, c0:c0 + GROUPS * P].reshape(2, 4, P, 2, S).transpose(3, 0, 2, 1, 4).reshape(4, P, TILE)
        c0 += GROUPS * P
        branch = (inp["w_branch_a"][l][order], inp["w_branch_b"][l], inp["w_branch_c"][l])
        for hf in range(2):
            for br in range(BR):
                t0 = T_MIX + hf * MIX_HALF + br * 6
                o[t0:t0 + 4] = cols(w, c0 + br * D + hf * HALF_N, 4)
                wb = branch[br][:, hf * HALF_N:(hf + 1) * HALF_N]
                o[t0 + 4:t0 + 6] = wb.reshape(4, P, 2, S).transpose(2, 1, 0, 3).reshape(2, P, TILE)
        o[T_WO:T_WQ] = inp["w_out"][l].reshape(4, 2, P, 2, HALF_N).transpose(3, 0, 2, 1, 4).reshape(8, P, TILE)
        o[T_WQ:T_UV] = cols(inp["peer_w_query"][l], 0, 2 * PH)
        u = inp["peer_expert_u"][l].reshape(NK, NK, KD, P)
        v = inp["peer_expert_v"][l].reshape(NK, NK, D)
        u = u.transpose(1, 3, 2, 0).reshape(NK, P, TILE)
        v = v.transpose(1, 0, 2)
        o[T_UV] = u[0]
        o[T_UV + 1:NT - 1:2] = u[1:]
        o[T_UV + 2:NT - 1:2] = v[:-1]
        o[NT - 1] = v[-1]
    return out.reshape(DEPTH * NT, P, TILE)


def kernel(**inputs):
    import concourse.bacc as bacc
    from concourse.bass_utils import run_bass_kernel_spmd

    inp = {k: np.ascontiguousarray(a) for k, a in inputs.items()}
    arrays = {
        "x": inp["x"],
        "stream": lay_out(inp),
        "consts": shape_constants(),
        "rel_bias": inp["rel_bias"],
        "final_gain": np.ascontiguousarray(np.broadcast_to(inp["final_gain"][None], (P, D))),
    }
    nc = bacc.Bacc("TRN2", target_bir_lowering=False, num_devices=1)
    args = [nc.dram_tensor(f"in_{n}", a.shape, mybir.dt.from_np(a.dtype), kind="ExternalInput").ap()
            for n, a in arrays.items()]
    out = nc.dram_tensor("out_y", (1, S, D), F32, kind="ExternalOutput").ap()
    program(nc, *args, out)
    r = run_bass_kernel_spmd(nc, [{f"in_{n}": a for n, a in arrays.items()}], core_ids=[0])
    return r.results[0]["out_y"]
```

```python
from contextlib import ExitStack

import numpy as np
import concourse.bass as bass
from concourse import mybir

F32 = mybir.dt.float32
F32R = mybir.dt.float32r
U32 = mybir.dt.uint32
ALU = mybir.AluOpType
ACT = mybir.ActivationFunctionType
AX = mybir.AxisListType

P = 128
D = 1024
KD = D // P
S = 256
TT = S // P
DEPTH = 2
HEADS, HD = 8, 64
QC = HEADS * HD // P
WINDOW = 128
BUCKETS, MAX_DIST = 32, 128
GROUPS = 4
POOL_WINDOWS = (2, 4, 8, 16)
PAD = 16
BR = 3
PH, TOPK, NK = 8, 16, 128
HALF_N = 512
EPS = 1e-6
NEG = -1e30
LOW = -3e38

TILE = 1024
RING = 4
STEPS = 4
BODY = 8
T_PARAM = 0
T_Q = T_PARAM + 2
T_K = T_Q + QC
T_V = T_K + 1
T_PZ = T_V + 1
T_GU = T_PZ + GROUPS
T_GV = T_GU + GROUPS
T_MIX = T_GV + 4
MIX_HALF = BR * 6
T_WO = T_MIX + 2 * MIX_HALF
T_WQ = T_WO + 8
T_PU = T_WQ + 2 * PH
PARKED = 40
T_PV = T_PU + PARKED
T_MU = T_PV + PARKED
NT = T_PU + 2 * NK
assert T_PU % RING == 0 and PARKED % RING == 0 and NK % RING == 0 and RING == 4
MAIN = NK - PARKED
LOP = T_PV + MAIN
TERMS = ((0, 0), (0, 1), (1, 0))

C_SK = 0
C_WPOOL = C_SK + 2 * NK
C_WSP = C_WPOOL + GROUPS * P
C_AGAIN = C_WSP + GROUPS * P
C_FGAIN = C_AGAIN + KD
C_BGATE = C_FGAIN + KD
C_PSCALE = C_BGATE + BR * KD
C_VGAIN = C_PSCALE + GROUPS
C_SINK = C_VGAIN + GROUPS
C_BSP = C_SINK + HEADS
C_END = C_BSP + GROUPS * P
assert C_END <= 2 * TILE

K_ID = 0
K_IOTA = K_ID + P
K_CINV = K_IOTA + P
K_TRIL = K_CINV + GROUPS * S
K_OH = K_TRIL + P
NDIST = 2 * P + P - 1
K_END = K_OH + NDIST

PLAN = (
    [("h1T", "V")] * 4 + [("q", "A")] * 2 + [("kv", "A")] + [("lg0", "V")] * 2 + [("lg1", "V")] * 4
    + [("pz", "V")] * 2 + [("gu", "A")] * 2 + [("gv", "A")] * 2 + [("pT0", "A")] * 2 + [("pT1", "A")] * 4
    + [("attn", "A")] * 4 + [("pool", "V")] * 2 + [("gmlp", "V")] * 2
    + ([("gate", "A")] * 2 + [("branch", "V")] * 2) * (2 * BR)
    + [("wo", "V")] * 4 + [("h2T", "V")] * 4 + [("qq", "A")] * 8 + [("score", "A")] * 8 + [("sel", "A")] * 2
)
NG = len(PLAN)
NBANK = 8
NGV = sum(who == "V" for _, who in PLAN)
NGA = NG - NGV
NCHAIN = 61
NSCAL = 8


def taken_before(group):
    return (sum(who == "V" for _, who in PLAN[:group]), sum(who == "A" for _, who in PLAN[:group]))


def bank_of(group):
    late = first("qq")
    return group % NBANK if group < late else 4 + (group - late) % 4


def last_in_bank(group):
    if group >= first("qq"):
        return group - 4 if group - 4 >= first("qq") else None
    return group - NBANK if group >= NBANK else None


def first(name):
    return [n for n, _ in PLAN].index(name)


def program(nc, x_in, stream, consts_in, rel_in, fgain_in, out):
    ctx = ExitStack()
    with ctx:
        def sb(name, shape, dt=F32):
            return ctx.enter_context(nc.sbuf_tensor(name, shape, dt))

        def sem(name):
            return ctx.enter_context(nc.semaphore(name))

        area_base = -(-nc.sbuf_base // 32) * 32
        area = sb("area", [P, S * NK])
        assert nc.sbuf_base == area_base + 4 * S * NK
        ring = sb("ring", [P, RING, TILE])
        halves = sb("halves", [P, RING, 2, TILE], F32R)
        x = sb("x", [P, TT, D])
        hT = sb("hT", [P, 2, KD, S], F32R)
        act = sb("act", [P, 2, S])
        coef_base = -(-nc.sbuf_base // 32) * 32
        coef = sb("coef", [P, 2, 2, S], F32R)
        assert nc.sbuf_base == coef_base + 4 * 2 * 2 * S
        ids = sb("ids", [P, 2 * P])
        stat = sb("stat", [P, 16])
        used = [0]

        def part(*shape, dt=F32, at=None):
            n = int(np.prod(shape))
            a = used[0] if at is None else at
            if at is None:
                used[0] += n
            v = area[:, a:a + n]
            if dt != F32:
                v = v.bitcast(dt)
            if len(shape) == 1:
                return v
            names = [f"a{i}" for i in range(len(shape))]
            return v.rearrange(f"p ({' '.join(names)}) -> p {' '.join(names)}", **dict(zip(names[1:], shape[1:])))

        def halves_part(name, *shape):
            a = used[0]
            used[0] = a + 2 * int(np.prod(shape))
            return nc.alloc_sbuf_tensor_at(name, [P, 2, *shape], F32R, offset=area_base + 4 * a)

        gates_t = area[:, :].rearrange("p (e t) -> p e t", t=S)
        par = part(2 * TILE)
        bias_at = used[0]
        bias = part(HEADS, 2 * P)
        maps = part(GROUPS * S + P)
        mixed_h = [halves_part(f"{n}_halves", 4, S) for n in ("attn", "pool", "gmlp")]
        turned = part(4, 4, P, at=used[0])
        merged_h = halves_part("merged_halves", KD, S)
        hn_at = used[0]
        hn = part(TT, D)
        lg1 = part(HEADS, 2 * P, at=hn_at)
        qT_at = used[0]
        qT = part(QC, S)
        kT = part(S)
        v_tok = part(TT, P)
        lg0 = part(HEADS, P)
        pT0 = part(HEADS, P)
        pT1 = part(HEADS * 2, P, at=bias_at)
        attnT = part(QC, S, at=qT_at)
        zp = part(GROUPS, PAD + S)
        pooled_at = used[0]
        win = [part(GROUPS, PAD + S) for _ in POOL_WINDOWS]
        dT = part(GROUPS, S)
        poolT = part(GROUPS, S)
        uT = part(GROUPS, S)
        gv = part(TT, GROUPS * P)
        gmT = part(GROUPS, S)
        wsp = part(GROUPS, P)
        sig = part(2, 4, S, at=pooled_at)
        mergedT = part(KD, S, at=pooled_at + 2 * 4 * S)
        small = part(64)
        used_mix = used[0]
        used[0] = 2 * TILE
        qqT = part(PH, 2, S)
        used[0] = max(used[0], PARKED * S)
        row = part(TT, PH, 2, NK)
        val = part(TT, PH, 2, TOPK)
        idx = part(TT, PH, 2, TOPK, dt=U32)
        idf = part(TT, PH, 2, TOPK)
        cand = part(TT, PH, TOPK, TOPK)
        top = part(TT, PH, TOPK)
        ci = part(TT, PH, TOPK, dt=U32)
        ca = part(TT, PH, TOPK, dt=U32)
        cb = part(TT, PH, TOPK, dt=U32)
        caf = part(TT, PH, TOPK)
        cbf = part(TT, PH, TOPK)
        eq = part(PH, TOPK, TOPK)
        sel = part(3, TT, P)
        used[0] = max(used[0], used_mix)
        assert used[0] <= S * NK, used[0]
        x_row = x[:, :, :].rearrange("p t d -> p (t d)")
        selT = x_row[:, 0:3 * S].rearrange("p (c t) -> p c t", c=3)
        onehot1 = x_row[:, 3 * S:7 * S].rearrange("p (s u k) -> p s u k", s=STEPS, u=2)
        onehot2 = nc.alloc_sbuf_tensor_at("onehot2", [P, STEPS, 2, NK], F32, offset=coef_base)

        bank = [ctx.enter_context(nc.psum_tensor(f"bank{i}", [P, HALF_N], F32)) for i in range(NBANK)]
        acc = bank[0:4]
        bank_g = bank[4:8]
        bank_u = bank[6:8]
        act_row = act[:, :, :].rearrange("p s t -> p (s t)")
        relx = act_row[0:BUCKETS + 1, 0:HEADS]
        relv = act_row[0:HEADS, HEADS:HEADS + NDIST]
        oh = area[0:BUCKETS + 1, S * NK - NDIST:S * NK]
        scratch = nc.dram_tensor("rel_scratch", (HEADS, P, NDIST), F32).ap()

        ident = ids[:, K_ID:K_ID + P]
        iota = ids[:, K_IOTA:K_IOTA + P]
        cinv = maps[:, 0:GROUPS * S].rearrange("p (g t) -> p g t", g=GROUPS)
        tril = maps[:, GROUPS * S:]

        loaded = [sem(f"loaded{i}") for i in range(RING)]
        tiles_used = sem("tiles_used")
        x_loaded = sem("x_loaded")
        consts_loaded = sem("consts_loaded")
        rel_loaded = sem("rel_loaded")
        rel_low = sem("rel_low")
        rel_product = sem("rel_product")
        rel_vector = sem("rel_vector")
        rel_written = sem("rel_written")
        bias_loaded = sem("bias_loaded")
        maps_loaded = sem("maps_loaded")
        params_ready = sem("params_ready")
        hi_done = sem("hi_done")
        lo_pool = sem("lo_pool")
        lo_vector = sem("lo_vector")
        mixed_ready = sem("mixed_ready")
        scaled = sem("scaled")
        wsp_ready = sem("wsp_ready")
        sumsq_ready = sem("sumsq_ready")
        root_ready = sem("root_ready")
        rstd_ready = sem("rstd_ready")
        hn_ready = sem("hn_ready")
        groups_done = sem("groups_done")
        taken_v = sem("taken_v")
        taken_a = sem("taken_a")
        chain = sem("chain")
        scal = sem("scal")
        max_ready = sem("max_ready")
        exp_ready = sem("exp_ready")
        probs_ready = sem("probs_ready")
        diff_ready = sem("diff_ready")
        vhat_ready = sem("vhat_ready")
        gm_ready = sem("gm_ready")
        merged_ready = sem("merged_ready")
        shifted_ready = sem("shifted_ready")
        gexp_ready = sem("gexp_ready")
        sel_ready = sem("sel_ready")
        square_done = sem("square_done")
        onehot_ready = sem("onehot_ready")
        onehots_ready = sem("onehots_ready")
        outer_done = sem("outer_done")
        table_ready = sem("table_ready")
        act_done = sem("act_done")
        parked_ready = sem("parked_ready")
        product_ready = sem("product_ready")
        coef_hi = sem("coef_hi")
        coef_ready = sem("coef_ready")
        x_updated = sem("x_updated")
        fgain_loaded = sem("fgain_loaded")
        out_ready = sem("out_ready")
        out_written = sem("out_written")

        NQ = S // 2

        block = ctx.enter_context(nc.Block())

        @block.sync
        def _(sp):
            sp.dma_start(x[:, :, :], x_in.rearrange("b (t p) d -> p (b t) d", p=P)).then_inc(x_loaded, 16)
            sp.dma_start(ids[:, :], consts_in[:, 0:2 * P]).then_inc(consts_loaded, 16)
            sp.dma_start(oh, consts_in[0:BUCKETS + 1, K_OH:K_END]).then_inc(rel_loaded, 16)
            sp.dma_start(relx[0:BUCKETS, :], rel_in).then_inc(rel_loaded, 16)

            def load(n, s, l):
                sp.dma_start(ring[:, s, :], stream[bass.ds(l * NT + n, 1)].rearrange("a p c -> (a p) c"))\
                    .then_inc(loaded[s], 16)

            with sp.Fori(0, DEPTH) as l:
                sp.wait_ge(lo_pool, l * LOP + 1)
                sp.wait_ge(lo_vector, l * NK + 1)
                for s in range(RING):
                    load(s, s, l)
                sp.wait_ge(params_ready, l + 1)
                sp.dma_start(maps, consts_in[:, K_CINV:K_OH]).then_inc(maps_loaded, 16)
                sp.wait_ge(rel_written, 16)
                sp.dma_start(bias, bass.AP(scratch.tensor, P - 1, [[NDIST - 1, P], [P * NDIST, HEADS], [1, 2 * P]]))\
                    .then_inc(bias_loaded, 16)
                with sp.Fori(1, T_PV // RING + 1) as r:
                    for s in range(RING):
                        sp.wait_ge(lo_pool, l * LOP + r * RING + (s - RING + 2))
                        load(r * RING + s, s, l)
                with sp.Fori(1, PARKED // RING + 1) as r:
                    for s in range(RING):
                        sp.wait_ge(lo_vector, l * NK + r * RING + (s - RING + 2))
                        load(r * RING + (T_PV + s), s, l)
                for s in range(RING):
                    if s in (0, 1, 3):
                        sp.wait_ge(lo_pool, l * LOP + (T_PV + 1 + (1, 2, 0, 3)[s]))
                    else:
                        sp.wait_ge(lo_vector, l * NK + (PARKED + 2))
                    load(T_MU + RING + s, s, l)
                with sp.Fori(2, 2 * MAIN // RING) as r:
                    for s in range(RING):
                        if s % 2:
                            sp.wait_ge(lo_pool, l * LOP + r * 2 + (T_PV + 1 + (s - 1) // 2))
                        else:
                            sp.wait_ge(lo_vector, l * NK + r * 2 + (PARKED - 1 + s // 2))
                        load(r * RING + (T_MU + s), s, l)
            sp.wait_ge(x_updated, 2 * DEPTH)
            sp.dma_start(ring[:, 0, :], fgain_in).then_inc(fgain_loaded, 16)
            sp.wait_ge(out_ready, TT)
            sp.dma_start(out.rearrange("b (t p) d -> p (b t) d", p=P), x[:, :, :]).then_inc(out_written, 16)
            sp.wait_ge(out_written, 16)

        @block.gpsimd
        def _(pool):
            pool.memset(relx[BUCKETS:BUCKETS + 1, :], NEG).then_inc(rel_low, 1)
            pool.wait_ge(rel_low, 1)
            pool.wait_ge(rel_vector, 1)
            pool.dma_start(scratch, relv.unsqueeze(1).to_broadcast([HEADS, P, NDIST])).then_inc(rel_written, 16)
            pool.wait_ge(consts_loaded, 16)
            pool.sem_inc(lo_pool, 1)

            def low(n, s, l):
                pool.wait_ge(hi_done, l * (NT - 2) + n - 1)
                pool.tensor_tensor(halves[:, s, 1, :], ring[:, s, :], halves[:, s, 0, :].bitcast(F32), ALU.subtract)\
                    .then_inc(lo_pool, 1)

            with pool.Fori(0, DEPTH) as l:
                pool.wait_ge(params_ready, l + 1)
                pool.sem_inc(lo_pool, 2)
                low(2, 2, l)
                low(3, 3, l)
                pool.wait_ge(maps_loaded, l * 16 + 16)
                for g in range(GROUPS):
                    i = pool.tensor_tensor(wsp[:, g, :], par[:, C_WSP + g * P:C_WSP + (g + 1) * P], tril, ALU.mult)
                i.then_inc(wsp_ready, 1)
                with pool.Fori(1, T_PV // RING) as r:
                    for s in range(RING):
                        low(r * RING + s, s, l)
                low(T_MU, 0, l)
                with pool.Fori(0, (MAIN - 1) // 2) as r:
                    low(r * 4 + (T_MU + 1), 1, l)
                    low(r * 4 + (T_MU + 3), 3, l)
                low(NT - 3, 1, l)

        @block.scalar
        def _(a):
            eps = stat[:, 15:16]
            one = stat[:, 12:13]

            def norm_sums(l, count, half):
                for t in range(TT):
                    i = a.activation(hn[:, t, :], x[:, t, :], ACT.Square, accum_out=stat[:, t:t + 1])
                    i.then_inc(scal, 1)
                a.wait_ge(scal, l * NSCAL + count + TT)
                a.activation(stat[:, 2:4], stat[:, 0:2], ACT.Sqrt, bias=eps, scale=1.0 / D).then_inc(root_ready, 1)
                a.wait_ge(rstd_ready, l * 3 + (1 if half == 0 else 3))
                for t in range(TT):
                    a.activation(hn[:, t, :], x[:, t, :], ACT.Copy, scale=stat[:, 4 + t:5 + t]).then_inc(hn_ready, 1)

            a.wait_ge(x_loaded, 16)
            a.wait_ge(chain, 1)
            with a.Fori(0, DEPTH) as l:
                g = [0]
                next_tile = [2]

                def high(n, s):
                    a.wait_ge(loaded[s], l * (16 * NT // RING) + (n - s) * (16 // RING) + 16)
                    a.activation(halves[:, s, 0, :], ring[:, s, :], ACT.Copy).then_inc(hi_done, 1)

                def high_up_to(last):
                    while next_tile[0] <= last:
                        n = next_tile[0]
                        if n >= RING:
                            a.wait_ge(tiles_used, l * NT + (n - RING + 1))
                        high(n, n % RING)
                        next_tile[0] += 1

                def group(name):
                    while PLAN[g[0]][1] != "A":
                        g[0] += 1
                    assert PLAN[g[0]][0] == name, (PLAN[g[0]], name)
                    a.wait_ge(groups_done, l * NG + (g[0] + 1))
                    g[0] += 1
                    return bank[bank_of(g[0] - 1)]

                a.wait_ge(x_updated, l * 2)
                for n in range(2):
                    a.wait_ge(loaded[n], l * (16 * NT // RING) + 16)
                    a.activation(par[:, n * TILE:(n + 1) * TILE], ring[:, n, :], ACT.Copy).then_inc(scal, 1)
                a.wait_ge(scal, l * NSCAL + 2)
                a.sem_inc(params_ready, 1)
                norm_sums(l, 2, 0)
                high_up_to(RING - 1)
                for n in range(2):
                    high_up_to(T_Q + 2 * n + 1 + 3)
                    b = group("q")
                    a.activation(qT[:, 2 * n:2 * n + 2, :], b[:, :].rearrange("p (c t) -> p c t", c=2), ACT.Copy)\
                        .then_inc(taken_a, 1)
                high_up_to(T_V + 3)
                b = group("kv")
                a.activation(kT, b[:, 0:S], ACT.Copy)
                a.activation(v_tok, b[:, S:].rearrange("p (t c) -> p t c", t=TT), ACT.Copy).then_inc(taken_a, 1)
                high_up_to(T_PZ + 3)
                for n in range(2):
                    high_up_to(T_GU + 2 * n + 1 + 3)
                    b = group("gu")
                    a.activation(uT[:, 2 * n:2 * n + 2, :], b[:, :].rearrange("p (c t) -> p c t", c=2),
                                 ACT.Gelu_apprx_tanh).then_inc(taken_a, 1)
                for t in range(TT):
                    high_up_to(T_GV + 3 + 3)
                    b = group("gv")
                    a.activation(gv[:, t, :], b[:, :], ACT.Gelu_apprx_tanh).then_inc(taken_a, 1)
                a.wait_ge(taken_a, l * NGA + 7)
                for t in range(TT):
                    a.activation(attnT[:, 2 * t:2 * t + 2, :], gv[:, t, :].rearrange("p (c t) -> p c t", c=2), ACT.Square, accum_out=stat[:, 6 + t:7 + t])\
                        .then_inc(scal, 1)
                a.wait_ge(scal, l * NSCAL + 6)
                a.activation(stat[:, 8:10], stat[:, 6:8], ACT.Sqrt, bias=eps, scale=1.0 / (GROUPS * P))\
                    .then_inc(root_ready, 1)
                for blk, lg in ((0, lg0), (1, lg1)):
                    a.wait_ge(max_ready, l * 2 + (blk + 1))
                    for h in range(HEADS):
                        a.activation(lg[:, h, :], lg[:, h, :], ACT.Exp, bias=small[:, blk * 32 + h:blk * 32 + h + 1],
                                     accum_out=small[:, blk * 32 + 16 + h:blk * 32 + 17 + h])
                    a.activation(small[:, blk * 32 + 24:blk * 32 + 32], small[:, blk * 32 + 8:blk * 32 + 16], ACT.Exp)\
                        .then_inc(exp_ready, 1)
                for n in range(2):
                    b = group("pT0")
                    a.activation(pT0[:, 4 * n:4 * n + 4, :], b[:, :].rearrange("p (c t) -> p c t", c=4), ACT.Copy)\
                        .then_inc(taken_a, 1)
                for n in range(4):
                    b = group("pT1")
                    a.activation(pT1[:, 4 * n:4 * n + 4, :], b[:, :].rearrange("p (c t) -> p c t", c=4), ACT.Copy)\
                        .then_inc(taken_a, 1)
                for c in range(QC):
                    b = group("attn")
                    a.activation(attnT[0:HD, c, :], b[0:HD, 0:S], ACT.Copy)
                    a.activation(attnT[HD:P, c, :], b[HD:P, S:], ACT.Copy).then_inc(taken_a, 1)
                for hf in range(2):
                    for br in range(BR):
                        if 3 * hf + br >= 2:
                            a.wait_ge(taken_v, l * NGV + taken_before(first("gate") + 4 * (3 * hf + br - 1))[0])
                        for n in range(2):
                            high_up_to(T_MIX + 6 * (3 * hf + br) + 2 * n + 1 + 3)
                            b = group("gate")
                            for c in range(2):
                                col = C_BGATE + br * KD + hf * 4 + 2 * n + c
                                i = a.activation(sig[:, (3 * hf + br) % 2, 2 * n + c, :], b[:, c * S:(c + 1) * S],
                                                 ACT.Sigmoid, bias=par[:, col:col + 1])
                            i.then_inc(taken_a, 1)
                high_up_to(T_WO + 7 + 3)
                a.wait_ge(x_updated, l * 2 + 1)
                norm_sums(l, 6, 1)
                for h in range(PH):
                    high_up_to(T_WQ + 2 * h + 1 + 3)
                    b = group("qq")
                    a.activation(qqT[:, h], b[:, :].rearrange("p (c t) -> p c t", c=2), ACT.Copy).then_inc(taken_a, 1)
                for n in range(8):
                    b = group("score")
                    a.activation(row[:, n // 4, 2 * (n % 4):2 * (n % 4) + 2].rearrange("p h c k -> p (h c k)"),
                                 b[:, :], ACT.Copy).then_inc(taken_a, 1)
                def gelu(o, s):
                    a.activation(o, bank_u[s][:, 0:S], ACT.Gelu_apprx_tanh).then_inc(act_done, 1)

                high_up_to(T_PU + RING - 1)
                a.activation(stat[:, 13:14], one, ACT.Gelu_apprx_tanh)
                with a.Fori(0, PARKED // RING) as r:
                    for s in range(RING):
                        a.wait_ge(tiles_used, l * NT + r * RING + (T_PU + s + 1))
                        high(r * RING + (T_PU + RING + s), s)
                        gelu(gates_t[:, bass.ds(r * RING + s, 1), :].rearrange("p e t -> p (e t)"), s % 2)
                a.wait_ge(shifted_ready, l + 1)
                a.activation(sel[:, 2], sel[:, 2], ACT.Exp).then_inc(gexp_ready, 1)
                for t in range(TT):
                    b = group("sel")
                    a.activation(selT[:, :, t * P:(t + 1) * P], b[:, 0:3 * P].rearrange("p (c t) -> p c t", c=3),
                                 ACT.Copy).then_inc(taken_a, 1)
                a.wait_ge(taken_a, l * NGA + NGA)

                def square(q, s, reuse):
                    if reuse:
                        a.wait_ge(outer_done, l * NQ + q - (STEPS - 1))
                    a.activation(onehot1[:, s, 1, :], iota, ACT.Square, bias=selT[:, 0, bass.ds(q * 2 + 1, 1)], scale=-1.0)\
                        .then_inc(square_done, 1)

                def onehot(q, s):
                    a.wait_ge(square_done, l * NQ + q + 1)
                    a.activation(onehot1[:, s, 1, :], onehot1[:, s, 1, :], ACT.Relu, bias=one, scale=-4.0)\
                        .then_inc(onehot_ready, 1)

                def table(q, s):
                    a.wait_ge(outer_done, l * NQ + q + 1)
                    a.activation(gates_t[:, PARKED:, bass.ds(q * 2, 2)],
                                 bank_g[s][:, 0:2 * NK].rearrange("p (t e) -> p e t", t=2)[:, PARKED:, :], ACT.Copy)\
                        .then_inc(table_ready, 1)

                for q in range(BODY):
                    if q >= 3:
                        table(q - 3, (q - 3) % STEPS)
                    square(q, q % STEPS, q >= STEPS)
                    if q >= 1:
                        onehot(q - 1, (q - 1) % STEPS)
                with a.Fori(1, NQ // BODY) as j:
                    for s in range(BODY):
                        table(j * BODY + (s - 3), (s - 3) % STEPS)
                        square(j * BODY + s, s % STEPS, True)
                        onehot(j * BODY + (s - 1), (s - 1) % STEPS)
                onehot(NQ - 1, STEPS - 1)
                for q in (NQ - 3, NQ - 2, NQ - 1):
                    table(q, q % STEPS)
                with a.Fori(0, PARKED // RING) as r:
                    for s in range(RING):
                        a.wait_ge(tiles_used, l * NT + r * RING + (T_PV + s + 1))
                        high(r * RING + (T_PV + RING + s), s)

                def main(p, s, block=None, last=False):
                    a.wait_ge(tiles_used, l * NT + p + (T_MU + 1))
                    if not last:
                        high(p + (T_MU + RING), s)
                    if block is not None:
                        k = 1 if s == 1 else 0
                        a.wait_ge(coef_ready, l * NK + block - 1)
                        gelu(act[:, k, :], k)

                main(0, 0, PARKED)
                with a.Fori(0, MAIN // 2 - 2) as r:
                    main(r * 4 + 1, 1, r * 2 + (PARKED + 1))
                    main(r * 4 + 2, 2)
                    main(r * 4 + 3, 3, r * 2 + (PARKED + 2))
                    main(r * 4 + 4, 0)
                end = 2 * MAIN - 7
                main(end, 1, NK - 3)
                main(end + 1, 2)
                main(end + 2, 3, NK - 2)
                main(end + 4, 1, NK - 1, last=True)
            a.wait_ge(x_updated, 2 * DEPTH)
            for t in range(TT):
                a.activation(hn[:, t, :], x[:, t, :], ACT.Square, accum_out=stat[:, t:t + 1]).then_inc(scal, 1)
            a.wait_ge(scal, NSCAL * DEPTH + TT)
            a.activation(stat[:, 2:4], stat[:, 0:2], ACT.Sqrt, bias=eps, scale=1.0 / D).then_inc(root_ready, 1)
            a.wait_ge(rstd_ready, 3 * DEPTH + 1)
            for t in range(TT):
                a.activation(hn[:, t, :], x[:, t, :], ACT.Copy, scale=stat[:, 4 + t:5 + t]).then_inc(hn_ready, 1)

        @block.vector
        def _(v):
            v.memset(stat[:, 12:13], 1.0)
            v.memset(stat[:, 15:16], EPS).then_inc(chain, 1)
            v.sem_inc(lo_vector, 1)
            v.wait_ge(rel_product, 1)
            v.tensor_copy(relv, bank[0][0:HEADS, 0:NDIST]).then_inc(rel_vector, 1)

            with v.Fori(0, DEPTH) as l:
                links = [1]

                def link(ins):
                    links[0] += 1
                    ins.then_inc(chain, 1)
                    v.wait_ge(chain, l * NCHAIN + links[0])

                g = [0]

                def group(name):
                    while PLAN[g[0]][1] != "V":
                        g[0] += 1
                    assert PLAN[g[0]][0] == name, (PLAN[g[0]], name)
                    v.wait_ge(groups_done, l * NG + (g[0] + 1))
                    g[0] += 1
                    return bank[bank_of(g[0] - 1)]

                def halve(halves, full):
                    link(v.tensor_copy(halves[0], full))
                    return v.tensor_tensor(halves[1], full, halves[0].bitcast(F32), ALU.subtract)

                def transposed(name, col):
                    for t in range(TT):
                        for n in range(2):
                            b = group(name)
                            i = v.tensor_tensor(
                                turned[:, 2 * t + n], b[:, :].rearrange("p (k t) -> p k t", k=4),
                                par[:, col + 4 * n:col + 4 * n + 4].unsqueeze(2).to_broadcast([P, 4, P]), ALU.mult)
                            i.then_inc(taken_v, 1)
                    v.wait_ge(taken_v, l * NGV + taken_before(g[0])[0])
                    for n in range(2):
                        for t in range(TT):
                            i = v.tensor_copy(hT[:, 0, 4 * n:4 * n + 4, t * P:(t + 1) * P], turned[:, 2 * t + n])
                    link(i)
                    for n in range(2):
                        for t in range(TT):
                            hi, lo = (hT[:, c, 4 * n:4 * n + 4, t * P:(t + 1) * P] for c in range(2))
                            i = v.tensor_tensor(lo, turned[:, 2 * t + n], hi.bitcast(F32), ALU.subtract)
                    i.then_inc(scaled, 1)

                def rstd(n, at, to):
                    v.wait_ge(root_ready, l * 3 + n)
                    v.reciprocal(stat[:, to:to + 2], stat[:, at:at + 2]).then_inc(rstd_ready, 1)

                rstd(1, 2, 4)
                v.wait_ge(params_ready, l + 1)
                transposed("h1T", C_AGAIN)
                v.wait_ge(bias_loaded, l * 16 + 16)
                for blk, lg, per in ((0, lg0, 4), (1, lg1, 2)):
                    for n in range(HEADS // per):
                        b = group(f"lg{blk}")
                        i = v.scalar_tensor_tensor(
                            lg[:, per * n:per * n + per, :], b[:, :].rearrange("p (h s) -> p h s", h=per), HD ** -0.5,
                            bias[:, per * n:per * n + per, (1 - blk) * P:], ALU.mult, ALU.add)
                        i.then_inc(taken_v, 1)
                    v.wait_ge(taken_v, l * NGV + (6 if blk == 0 else 10))
                    o = blk * 32
                    link(v.tensor_reduce(small[:, o:o + 8], lg, AX.X, ALU.max))
                    link(v.tensor_tensor(small[:, o:o + 8], small[:, o:o + 8], par[:, C_SINK:C_SINK + 8], ALU.max))
                    link(v.tensor_scalar(small[:, o:o + 8], small[:, o:o + 8], -1.0, None, ALU.mult))
                    v.tensor_tensor(small[:, o + 8:o + 16], small[:, o:o + 8], par[:, C_SINK:C_SINK + 8], ALU.add)\
                        .then_inc(max_ready, 1)
                v.wait_ge(maps_loaded, l * 16 + 16)
                link(v.memset(zp[:, :, 0:PAD], 0.0))
                for n in range(2):
                    b = group("pz")
                    v.tensor_copy(zp[:, 2 * n:2 * n + 2, PAD:], b[:, :].rearrange("p (c t) -> p c t", c=2))\
                        .then_inc(taken_v, 1)
                v.wait_ge(taken_v, l * NGV + 12)
                src = zp
                for n, w in enumerate(POOL_WINDOWS):
                    link(v.tensor_tensor(win[n][:, n:, w - 1:], src[:, n:, w - 1:],
                                         src[:, n:, w - 1 - w // 2:PAD + S - w // 2], ALU.add))
                    src = win[n]
                for n in range(GROUPS):
                    i = v.tensor_tensor(dT[:, n, :], win[n][:, n, PAD:], cinv[:, n, :], ALU.mult)
                link(i)
                v.tensor_tensor(dT, dT, zp[:, :, PAD:], ALU.subtract).then_inc(diff_ready, 1)
                rstd(2, 8, 10)
                v.wait_ge(rstd_ready, l * 3 + 2)
                for t in range(TT):
                    i = v.tensor_scalar(gv[:, t, :], gv[:, t, :], stat[:, 10 + t:11 + t], None, ALU.mult)
                i.then_inc(vhat_ready, 1)
                for blk, lg in ((0, lg0), (1, lg1)):
                    o = blk * 32
                    v.wait_ge(exp_ready, l * 2 + (blk + 1))
                    link(v.tensor_tensor(small[:, o + 16:o + 24], small[:, o + 16:o + 24], small[:, o + 24:o + 32], ALU.add))
                    link(v.reciprocal(small[:, o + 16:o + 24], small[:, o + 16:o + 24]))
                    v.tensor_tensor(lg, lg, small[:, o + 16:o + 24].unsqueeze(2).to_broadcast([P, HEADS, (blk + 1) * P]),
                                    ALU.mult).then_inc(probs_ready, 1)
                for n in range(2):
                    b = group("pool")
                    v.tensor_tensor(
                        poolT[:, 2 * n:2 * n + 2, :], b[:, :].rearrange("p (c t) -> p c t", c=2),
                        par[:, C_PSCALE + 2 * n:C_PSCALE + 2 * n + 2].unsqueeze(2).to_broadcast([P, 2, S]), ALU.mult,
                    ).then_inc(taken_v, 1)
                bsp = par[:, C_BSP:C_BSP + GROUPS * P].rearrange("p (g t) -> p g t", g=GROUPS)
                for n in range(2):
                    b = group("gmlp")
                    for c in range(2):
                        i = v.scalar_tensor_tensor(
                            gmT[:, 2 * n + c, :].rearrange("p (c t) -> p c t", c=2),
                            b[:, c * S:(c + 1) * S].rearrange("p (c t) -> p c t", c=2),
                            par[:, C_VGAIN + 2 * n + c:C_VGAIN + 2 * n + c + 1],
                            bsp[:, 2 * n + c, :].unsqueeze(1).to_broadcast([P, 2, P]), ALU.mult, ALU.add)
                    i.then_inc(taken_v, 1)
                v.wait_ge(taken_v, l * NGV + 16)
                v.wait_ge(taken_a, l * NGA + 5)
                link(v.tensor_tensor(gmT, gmT, uT, ALU.mult))
                v.wait_ge(taken_a, l * NGA + taken_before(first("gate"))[1])
                for m_h, m in zip(mixed_h, (attnT, poolT, gmT)):
                    halve((m_h[:, 0], m_h[:, 1]), m).then_inc(mixed_ready, 1)
                for hf in range(2):
                    for br in range(BR):
                        for n in range(2):
                            b = group("branch")
                            y = b[:, :].rearrange("p (c t) -> p c t", c=2)
                            m = mergedT[:, 4 * hf + 2 * n:4 * hf + 2 * n + 2, :]
                            s = sig[:, (3 * hf + br) % 2, 2 * n:2 * n + 2, :]
                            v.wait_ge(taken_a, l * NGA + taken_before(g[0])[1])
                            if br == 0:
                                v.tensor_tensor(m, s, y, ALU.mult).then_inc(taken_v, 1)
                            else:
                                tmp = zp[:, 2 * n:2 * n + 2, 0:S]
                                i = v.tensor_tensor(tmp, s, y, ALU.mult)
                                i.then_inc(taken_v, 1)
                                v.wait_ge(taken_v, l * NGV + taken_before(g[0])[0])
                                link(v.tensor_tensor(m, m, tmp, ALU.add))
                            if br == BR - 1:
                                c = slice(4 * hf + 2 * n, 4 * hf + 2 * n + 2)
                                halve((merged_h[:, 0, c], merged_h[:, 1, c]), m).then_inc(merged_ready, 1)
                for hf in range(2):
                    for t in range(TT):
                        b = group("wo")
                        xs = x[:, t, hf * HALF_N:(hf + 1) * HALF_N]
                        v.tensor_tensor(xs, xs, b[:, :], ALU.add).then_inc(taken_v, 1)
                v.wait_ge(taken_v, l * NGV + taken_before(first("h2T"))[0])
                v.sem_inc(x_updated, 1)
                rstd(3, 2, 4)
                transposed("h2T", C_FGAIN)

                def then_search(ins):
                    links[0] += 1
                    ins.then_inc(chain, 1)
                    v.wait_ge(chain, l * NCHAIN + links[0])
                    v.memset(stat[:, 14:15], 0.0)

                v.wait_ge(taken_a, l * NGA + NGA - 2)
                v.memset(stat[:, 14:15], 0.0)
                rows = [(t, h, c) for t in range(TT) for h in range(PH) for c in range(2)]
                for k in range(2):
                    for t, h, c in rows:
                        i = v.max(val[:, t, h, c, 8 * k:8 * k + 8], row[:, t, h, c, :])
                    then_search(i)
                    for t, h, c in rows:
                        i = v.max_index(idx[:, t, h, c, 8 * k:8 * k + 8], val[:, t, h, c, 8 * k:8 * k + 8], row[:, t, h, c, :])
                    then_search(i)
                    if k == 0:
                        for t, h, c in rows:
                            i = v.match_replace(row[:, t, h, c, :], val[:, t, h, c, 0:8], row[:, t, h, c, :], LOW)
                        then_search(i)
                v.tensor_copy(idf.rearrange("p a b c d -> p (a b c d)"), idx.rearrange("p a b c d -> p (a b c d)"))
                for t in range(TT):
                    i = v.tensor_tensor(cand[:, t], val[:, t, :, 0, :].unsqueeze(3).to_broadcast([P, PH, TOPK, TOPK]),
                                        val[:, t, :, 1, :].unsqueeze(2).to_broadcast([P, PH, TOPK, TOPK]), ALU.add)
                then_search(i)
                pairs = [(t, h) for t in range(TT) for h in range(PH)]
                for k in range(2):
                    ks = slice(8 * k, 8 * k + 8)
                    flat = [cand[:, t, h].rearrange("p a b -> p (a b)") for t, h in pairs]
                    for (t, h), f in zip(pairs, flat):
                        i = v.max(top[:, t, h, ks], f)
                    then_search(i)
                    for (t, h), f in zip(pairs, flat):
                        i = v.max_index(ci[:, t, h, ks], top[:, t, h, ks], f)
                    then_search(i)
                    if k == 0:
                        for (t, h), f in zip(pairs, flat):
                            i = v.match_replace(f, top[:, t, h, ks], f, LOW)
                        then_search(i)
                gate = sel[:, 2].rearrange("p t (h j) -> p t h j", h=PH)
                for t in range(TT):
                    i = v.tensor_tensor(gate[:, t], top[:, t], top[:, t, :, 0:1].to_broadcast([P, PH, TOPK]), ALU.subtract)
                i.then_inc(shifted_ready, 1)
                v.tensor_scalar(ca.rearrange("p t h j -> p (t h j)"), ci.rearrange("p t h j -> p (t h j)"), 4, None,
                                ALU.logical_shift_right)
                link(v.tensor_scalar(cb.rearrange("p t h j -> p (t h j)"), ci.rearrange("p t h j -> p (t h j)"), 15, None,
                                     ALU.bitwise_and))
                v.tensor_copy(caf, ca)
                link(v.tensor_copy(cbf, cb))
                for c, rank in ((0, caf), (1, cbf)):
                    for t in range(TT):
                        link(v.tensor_tensor(eq, rank[:, t].unsqueeze(3).to_broadcast([P, PH, TOPK, TOPK]),
                                             iota[:, 0:TOPK].unsqueeze(1).unsqueeze(1).to_broadcast([P, PH, TOPK, TOPK]),
                                             ALU.is_equal))
                        link(v.tensor_tensor(eq, eq, idf[:, t, :, c, :].unsqueeze(2).to_broadcast([P, PH, TOPK, TOPK]),
                                             ALU.mult))
                        link(v.tensor_reduce(sel[:, c, t].rearrange("p (h j) -> p h j", h=PH), eq, AX.X, ALU.add))
                v.wait_ge(gexp_ready, l + 1)
                gs = small[:, 0:16].rearrange("p (t h) -> p t h", t=TT)
                link(v.tensor_reduce(gs, gate, AX.X, ALU.add))
                link(v.reciprocal(gs, gs))
                for t in range(TT):
                    i = v.tensor_tensor(gate[:, t], gate[:, t], gs[:, t].unsqueeze(2).to_broadcast([P, PH, TOPK]), ALU.mult)
                i.then_inc(sel_ready, 1)
                v.wait_ge(taken_a, l * NGA + NGA)
                def onehots(q, s, reuse):
                    if reuse:
                        v.wait_ge(outer_done, l * NQ + q - (STEPS - 1))
                    for u in range(2):
                        key1, key2, weight = (selT[:, c, bass.ds(q * 2 + u, 1)] for c in range(3))
                        if u == 0:
                            v.tensor_scalar(onehot1[:, s, 0, :], iota, key1, None, ALU.is_equal)
                        i = v.tensor_scalar(onehot2[:, s, u, :], iota, key2, weight, ALU.is_equal, ALU.mult)
                    i.then_inc(onehots_ready, 1)

                def gate_parked(q, s):
                    v.wait_ge(table_ready, l * NQ + q + 1)
                    place = gates_t[:, 0:PARKED, bass.ds(q * 2, 2)]
                    v.tensor_tensor(place, bank_g[s][:, 0:2 * NK].rearrange("p (t e) -> p e t", t=2)[:, 0:PARKED, :],
                                    place, ALU.mult).then_inc(parked_ready, 1)

                v.wait_ge(act_done, l * NK + PARKED)
                for q in range(BODY):
                    onehots(q, q % STEPS, q >= STEPS)
                    if q >= 3:
                        gate_parked(q - 3, (q - 3) % STEPS)
                with v.Fori(1, NQ // BODY) as j:
                    for s in range(BODY):
                        onehots(j * BODY + s, s % STEPS, True)
                        gate_parked(j * BODY + (s - 3), (s - 3) % STEPS)
                for q in (NQ - 3, NQ - 2, NQ - 1):
                    gate_parked(q, q % STEPS)

                def low(b, n, s):
                    v.wait_ge(hi_done, l * (NT - 2) + n - 1)
                    v.tensor_tensor(halves[:, s, 1, :], ring[:, s, :], halves[:, s, 0, :].bitcast(F32), ALU.subtract)\
                        .then_inc(lo_vector, 1)

                def parked(b, k, s, reuse):
                    low(b, b + T_PV, s)
                    if reuse:
                        v.wait_ge(tiles_used, l * NT + b + (T_PV - 1))
                    full = gates_t[:, bass.ds(b, 1), :].rearrange("p e t -> p (e t)")
                    v.tensor_copy(coef[:, k, 0, :], full).then_inc(coef_hi, 1)
                    v.wait_ge(coef_hi, l * NK + b + 1)
                    v.tensor_tensor(coef[:, k, 1, :], full, coef[:, k, 0, :].bitcast(F32), ALU.subtract)\
                        .then_inc(coef_ready, 1)

                v.wait_ge(parked_ready, l * NQ + NQ)
                for b in range(RING):
                    parked(b, b % 2, b % RING, b >= 2)
                with v.Fori(1, PARKED // RING) as r:
                    for s in range(RING):
                        parked(r * RING + s, s % 2, s, True)

                def gated(b, k, n, s, used_at):
                    low(b, n, s)
                    v.wait_ge(act_done, l * NK + b + 1)
                    full = act[:, k, :]
                    v.tensor_tensor(full, full, gates_t[:, bass.ds(b, 1), :].rearrange("p e t -> p (e t)"),
                                    ALU.mult).then_inc(product_ready, 1)
                    v.wait_ge(product_ready, l * MAIN + b - (PARKED - 1))
                    v.wait_ge(tiles_used, l * NT + used_at)
                    v.tensor_copy(coef[:, k, 0, :], full).then_inc(coef_hi, 1)
                    v.wait_ge(coef_hi, l * NK + b + 1)
                    v.tensor_tensor(coef[:, k, 1, :], full, coef[:, k, 0, :].bitcast(F32), ALU.subtract)\
                        .then_inc(coef_ready, 1)

                v.wait_ge(table_ready, l * NQ + NQ)
                gated(PARKED, 0, T_MU + 2, 2, T_MU - 1)
                gated(PARKED + 1, 1, T_MU + 4, 0, T_MU)
                with v.Fori(1, MAIN // 2 - 1) as r:
                    for k in range(2):
                        gated(r * 2 + (PARKED + k), k, r * 4 + (T_MU + 2 + 2 * k), (2, 0)[k], r * 4 + (T_MU - 1 + 2 * k))
                gated(NK - 2, 0, NT - 2, 2, NT - 5)
                gated(NK - 1, 1, NT - 1, 3, NT - 3)
                v.wait_ge(tiles_used, l * NT + NT)
                for t in range(TT):
                    for hf in range(2):
                        i = v.tensor_copy(x[:, t, hf * HALF_N:(hf + 1) * HALF_N], acc[2 * t + hf][:, :])
                i.then_inc(x_updated, 1)
                v.wait_ge(x_updated, l * 2 + 2)
                assert links[0] == NCHAIN + 1, links[0]
            v.wait_ge(root_ready, 3 * DEPTH + 1)
            v.reciprocal(stat[:, 4:6], stat[:, 2:4]).then_inc(rstd_ready, 1)
            v.wait_ge(fgain_loaded, 16)
            for t in range(TT):
                v.wait_ge(hn_ready, 2 * TT * DEPTH + t + 1)
                v.tensor_tensor(x[:, t, :], hn[:, t, :], ring[:, 0, :], ALU.mult)\
                    .then_inc(out_ready, 1)

        @block.tensor
        def _(pe):
            pe.wait_ge(consts_loaded, 16)
            pe.wait_ge(rel_loaded, 32)
            pe.wait_ge(rel_low, 1)
            pe.matmul(bank[0][0:HEADS, 0:NDIST], relx, oh, start=True, stop=True).then_inc(rel_product, 1)
            pe.wait_ge(rel_vector, 1)

            with pe.Fori(0, DEPTH) as l:
                g = [0]

                def group(name):
                    assert PLAN[g[0]][0] == name, (PLAN[g[0]], name)
                    prev = last_in_bank(g[0])
                    if prev is not None:
                        tv, ta = taken_before(prev + 1)
                        if PLAN[prev][1] == "V":
                            pe.wait_ge(taken_v, l * NGV + tv)
                        else:
                            pe.wait_ge(taken_a, l * NGA + ta)
                    g[0] += 1
                    return bank[bank_of(g[0] - 1)]

                def tile(n, k):
                    pe.wait_ge(lo_pool, l * LOP + n + 2)
                    return halves[:, n % RING].rearrange("p h (k c) -> p h k c", k=k)

                def product(o, stationary, moving, begin=True, end=True):
                    for n, (a, b) in enumerate(TERMS):
                        i = pe.matmul(o, stationary[a], moving[b], start=begin and n == 0, stop=end and n == len(TERMS) - 1)
                        first_of = i if n == 0 else first_of
                    return first_of, i

                def columns(n, o):
                    w = tile(n, KD)
                    for k in range(KD):
                        one, i = product(o, (w[:, 0, k], w[:, 1, k]), (hT[:, 0, k], hT[:, 1, k]), k == 0, k == KD - 1)
                        if k == 0:
                            one.then_inc(tiles_used, 1)
                    return i

                def transpose_rows(name):
                    for t in range(TT):
                        for n in range(2):
                            b = group(name)
                            for k in range(4):
                                i = pe.transpose(b[:, k * P:(k + 1) * P], hn[:, t, (4 * n + k) * P:(4 * n + k + 1) * P], ident)
                            i.then_inc(groups_done, 1)

                pe.wait_ge(params_ready, l + 1)
                pe.sem_inc(tiles_used, 1)
                pe.wait_ge(hn_ready, l * 2 * TT + TT)
                transpose_rows("h1T")
                pe.wait_ge(scaled, l * 2 + 1)
                for n in range(QC // 2):
                    b = group("q")
                    for c in range(2):
                        i = columns(T_Q + 2 * n + c, b[:, c * S:(c + 1) * S])
                    i.then_inc(groups_done, 1)
                b = group("kv")
                columns(T_K, b[:, 0:S])
                w = tile(T_V, KD)
                for t in range(TT):
                    for k in range(KD):
                        rows = [hT[:, c, k, t * P:(t + 1) * P] for c in range(2)]
                        one, i = product(b[:, S + t * P:S + (t + 1) * P], rows, (w[:, 0, k], w[:, 1, k]), k == 0, k == KD - 1)
                        if t == 0 and k == 0:
                            one.then_inc(tiles_used, 1)
                i.then_inc(groups_done, 1)
                pe.wait_ge(taken_a, l * NGA + 3)
                for blk, per in ((0, 4), (1, 2)):
                    width = (blk + 1) * P
                    for n in range(HEADS // per):
                        b = group(f"lg{blk}")
                        for u in range(per):
                            h = per * n + u
                            rows = slice(0, HD) if h < 4 else slice(HD, P)
                            i = pe.matmul(b[:, u * width:(u + 1) * width], qT[rows, h % 4, blk * P:(blk + 1) * P],
                                          kT[rows, 0:width], start=True, stop=True)
                        i.then_inc(groups_done, 1)
                for name, t0 in (("pz", T_PZ), ("gu", T_GU)):
                    for n in range(GROUPS // 2):
                        b = group(name)
                        for c in range(2):
                            i = columns(t0 + 2 * n + c, b[:, c * S:(c + 1) * S])
                        i.then_inc(groups_done, 1)
                b = [group("gv") for _ in range(TT)]
                for c in range(2):
                    for kh in range(2):
                        w = tile(T_GV + 2 * c + kh, 4)
                        for t in range(TT):
                            for k in range(4):
                                rows = [hT[:, e, 4 * kh + k, t * P:(t + 1) * P] for e in range(2)]
                                one, i = product(b[t][:, c * S:(c + 1) * S], rows, (w[:, 0, k], w[:, 1, k]),
                                                 kh == 0 and k == 0, kh == 1 and k == 3)
                                if t == 0 and k == 0:
                                    one.then_inc(tiles_used, 1)
                            if c == 1 and kh == 1:
                                i.then_inc(groups_done, 1)
                pe.wait_ge(probs_ready, l * 2 + 1)
                for n in range(2):
                    b = group("pT0")
                    for u in range(4):
                        i = pe.transpose(b[:, u * P:(u + 1) * P], lg0[:, 4 * n + u, :], ident)
                    i.then_inc(groups_done, 1)
                pe.wait_ge(probs_ready, l * 2 + 2)
                for n in range(4):
                    b = group("pT1")
                    for u in range(4):
                        i = pe.transpose(b[:, u * P:(u + 1) * P], lg1[:, 2 * n + u // 2, (u % 2) * P:(u % 2 + 1) * P], ident)
                    i.then_inc(groups_done, 1)
                pe.wait_ge(taken_a, l * NGA + taken_before(first("attn"))[1])
                for c in range(QC):
                    b = group("attn")
                    for u in range(2):
                        h = c + 4 * u
                        pe.matmul(b[:, u * S:u * S + P], v_tok[:, 0, :], pT0[:, h, :], start=True, stop=True)
                        for sblk in range(2):
                            i = pe.matmul(b[:, u * S + P:(u + 1) * S], v_tok[:, sblk, :], pT1[:, 2 * h + sblk, :],
                                          start=sblk == 0, stop=sblk == 1)
                    i.then_inc(groups_done, 1)
                pe.wait_ge(diff_ready, l + 1)
                for n in range(2):
                    b = group("pool")
                    for c in range(2):
                        gg = 2 * n + c
                        i = pe.matmul(b[:, c * S:(c + 1) * S], par[:, C_WPOOL + gg * P:C_WPOOL + (gg + 1) * P], dT[:, gg, :],
                                      start=True, stop=True)
                    i.then_inc(groups_done, 1)
                pe.wait_ge(vhat_ready, l + 1)
                pe.wait_ge(wsp_ready, l + 1)
                for n in range(2):
                    b = group("gmlp")
                    for c in range(2):
                        gg = 2 * n + c
                        for t in range(TT):
                            i = pe.matmul(b[:, c * S + t * P:c * S + (t + 1) * P], gv[:, t, gg * P:(gg + 1) * P],
                                          wsp[:, gg, :], start=True, stop=True)
                    i.then_inc(groups_done, 1)
                pe.wait_ge(taken_a, l * NGA + taken_before(first("gate"))[1])
                for hf in range(2):
                    for br, mixed in enumerate(mixed_h):
                        t0 = T_MIX + hf * MIX_HALF + br * 6
                        for n in range(2):
                            b = group("gate")
                            for c in range(2):
                                i = columns(t0 + 2 * n + c, b[:, c * S:(c + 1) * S])
                            i.then_inc(groups_done, 1)
                        if hf == 0:
                            pe.wait_ge(mixed_ready, l * BR + br + 1)
                        for n in range(2):
                            b = group("branch")
                            w = tile(t0 + 4 + n, 4)
                            for c in range(2):
                                for k in range(4):
                                    part_w = [w[:, e, k, c * P:(c + 1) * P] for e in range(2)]
                                    one, i = product(b[:, c * S:(c + 1) * S], part_w, (mixed[:, 0, k], mixed[:, 1, k]),
                                                     k == 0, k == 3)
                                    if c == 0 and k == 0:
                                        one.then_inc(tiles_used, 1)
                            i.then_inc(groups_done, 1)
                for hf in range(2):
                    b = [group("wo") for _ in range(TT)]
                    for kq in range(4):
                        w = tile(T_WO + 4 * hf + kq, 2)
                        if hf == 0:
                            pe.wait_ge(merged_ready, l * 4 + kq + 1)
                        for t in range(TT):
                            for k in range(2):
                                rows = [merged_h[:, e, 2 * kq + k, t * P:(t + 1) * P] for e in range(2)]
                                one, i = product(b[t][:, :], rows, (w[:, 0, k], w[:, 1, k]), kq == 0 and k == 0,
                                                 kq == 3 and k == 1)
                                if t == 0 and k == 0:
                                    one.then_inc(tiles_used, 1)
                            if kq == 3:
                                i.then_inc(groups_done, 1)
                pe.wait_ge(hn_ready, l * 2 * TT + 2 * TT)
                transpose_rows("h2T")
                pe.wait_ge(scaled, l * 2 + 2)
                pe.wait_ge(taken_v, l * NGV + NGV)
                for t in range(TT):
                    for hf in range(2):
                        pe.matmul(acc[2 * t + hf][:, :], ident, x[:, t, hf * HALF_N:(hf + 1) * HALF_N], start=True,
                                  stop=True)
                for h in range(PH):
                    b = group("qq")
                    for c in range(2):
                        i = columns(T_WQ + 2 * h + c, b[:, c * S:(c + 1) * S])
                    i.then_inc(groups_done, 1)
                pe.wait_ge(taken_a, l * NGA + taken_before(first("score"))[1])
                for n in range(8):
                    b = group("score")
                    for u in range(2):
                        for c in range(2):
                            h, t = 2 * (n % 4) + u, n // 4
                            i = pe.matmul(b[:, (2 * u + c) * NK:(2 * u + c + 1) * NK], qqT[:, h, c, t * P:(t + 1) * P],
                                          par[:, C_SK + c * NK:C_SK + (c + 1) * NK], start=True, stop=True)
                    i.then_inc(groups_done, 1)
                def u_product(s, k, opens=False):
                    w = halves[:, s].rearrange("p h (k c) -> p h k c", k=KD)
                    for c in range(KD):
                        one, i = product(bank_u[k][:, 0:S], (w[:, 0, c], w[:, 1, c]), (hT[:, 0, c], hT[:, 1, c]), c == 0,
                                         c == KD - 1)
                        if opens and c == 0:
                            one.then_inc(tiles_used, 1)
                    i.then_inc(tiles_used, 1)

                def v_product(b, s, k):
                    pe.wait_ge(lo_vector, l * NK + b + 2)
                    pe.wait_ge(coef_ready, l * NK + b + 1)
                    for t in range(TT):
                        for a, e in TERMS:
                            for hf in range(2):
                                i = pe.matmul(acc[2 * t + hf][:, :], coef[:, k, a, t * P:(t + 1) * P],
                                              halves[:, s, e, hf * HALF_N:(hf + 1) * HALF_N], start=False, stop=True,
                                              skip_group_check=True)
                    i.then_inc(tiles_used, 1)

                pe.wait_ge(taken_a, l * NGA + NGA - 2)
                for s in range(RING):
                    pe.wait_ge(lo_pool, l * LOP + (T_PU + s + 2))
                    if s >= 2:
                        pe.wait_ge(act_done, l * NK + (s - 1))
                    u_product(s, s % 2, opens=s == 0)
                with pe.Fori(1, PARKED // RING) as r:
                    for s in range(RING):
                        pe.wait_ge(lo_pool, l * LOP + r * RING + (T_PU + s + 2))
                        pe.wait_ge(act_done, l * NK + r * RING + (s - 1))
                        u_product(s, s % 2)
                pe.wait_ge(sel_ready, l + 1)
                for t in range(TT):
                    b = group("sel")
                    for c in range(3):
                        i = pe.transpose(b[:, c * P:(c + 1) * P], sel[:, c, t, :], ident)
                    i.then_inc(groups_done, 1)
                assert g[0] == NG

                def outer(q, s, reuse):
                    pe.wait_ge(onehots_ready, l * NQ + q + 1)
                    pe.wait_ge(onehot_ready, l * NQ + q + 1)
                    if reuse:
                        pe.wait_ge(parked_ready, l * NQ + q - (STEPS - 1))
                    for u in range(2):
                        i = pe.matmul(bank_g[s][:, u * NK:(u + 1) * NK], onehot1[:, s, u, :], onehot2[:, s, u, :],
                                      start=True, stop=True)
                    i.then_inc(outer_done, 1)

                pe.wait_ge(taken_a, l * NGA + NGA)
                pe.wait_ge(act_done, l * NK + PARKED)
                for q in range(BODY):
                    outer(q, q % STEPS, q >= STEPS)
                with pe.Fori(1, NQ // BODY) as j:
                    for s in range(BODY):
                        outer(j * BODY + s, s % STEPS, True)

                with pe.Fori(0, PARKED // RING) as r:
                    for s in range(RING):
                        v_product(r * RING + s, s, s % 2)

                def u_main(b, s, k):
                    pe.wait_ge(lo_pool, l * LOP + b + (T_PV - PARKED + 2))
                    pe.wait_ge(act_done, l * NK + b - 1)
                    u_product(s, k)

                u_main(PARKED, 0, 0)
                with pe.Fori(0, MAIN // 2 - 1) as r:
                    u_main(r * 2 + (PARKED + 1), 1, 1)
                    v_product(r * 2 + PARKED, 2, 0)
                    u_main(r * 2 + (PARKED + 2), 3, 0)
                    v_product(r * 2 + (PARKED + 1), 0, 1)
                u_main(NK - 1, 1, 1)
                v_product(NK - 2, 2, 0)
                v_product(NK - 1, 3, 1)


def shape_constants():
    c = np.zeros((P, K_END), np.float32)
    c[:, K_ID:K_ID + P] = np.eye(P)
    c[:, K_IOTA:K_IOTA + P] = np.arange(P)
    for g, w in enumerate(POOL_WINDOWS):
        c[:, K_CINV + g * S:K_CINV + (g + 1) * S] = 1.0 / np.minimum(np.arange(1, S + 1), w)
    c[:, K_TRIL:K_TRIL + P] = np.triu(np.ones((P, P)))
    exact = BUCKETS // 2
    for j in range(NDIST):
        dist = 2 * P - 1 - j
        if dist >= WINDOW or dist < 0:
            b = BUCKETS
        elif dist < exact:
            b = dist
        else:
            b = min(BUCKETS - 1, exact + int(np.log(dist / exact) / np.log(MAX_DIST / exact) * (BUCKETS - exact)))
        c[b, K_OH + j] = 1.0
    return c


def lay_out(inp):
    w_in = inp["w_in"]
    n_q, n_kv = HEADS * HD, 2 * HD
    order = np.concatenate([np.r_[c * HD:(c + 1) * HD, (c + 4) * HD:(c + 5) * HD] for c in range(QC)])
    out = np.zeros((DEPTH, NT, P, TILE), np.float32)

    def cols(w, c0, n):
        return w[:, c0:c0 + n * P].reshape(KD, P, n, P).transpose(2, 1, 0, 3).reshape(n, P, TILE)

    for l in range(DEPTH):
        o, w = out[l], w_in[l]
        par = np.zeros((P, 2 * TILE), np.float32)
        par[:, C_SK:C_SK + NK] = inp["peer_sub_keys1"][l].T
        par[:, C_SK + NK:C_SK + 2 * NK] = inp["peer_sub_keys2"][l].T
        par[:, C_WPOOL:C_WPOOL + GROUPS * P] = inp["w_pool"][l].transpose(1, 0, 2).reshape(P, -1)
        par[:, C_WSP:C_WSP + GROUPS * P] = inp["w_spatial"][l].transpose(2, 0, 1).reshape(P, -1)
        for c, name, k in ((C_AGAIN, "attn_norm_gain", KD), (C_FGAIN, "ffn_norm_gain", KD), (C_BGATE, "b_gate", BR * KD),
                           (C_PSCALE, "pool_scale", GROUPS), (C_VGAIN, "gmlp_v_gain", GROUPS)):
            par[:, c:c + k] = inp[name][l].reshape(k, P).T
        par[:, C_SINK:C_SINK + HEADS] = inp["attn_sinks"][l][None]
        par[:, C_BSP:C_BSP + GROUPS * P] = inp["b_spatial"][l].reshape(1, -1)
        o[T_PARAM:T_Q] = par.reshape(P, 2, TILE).transpose(1, 0, 2)
        o[T_Q:T_K] = cols(w[:, order], 0, QC)
        o[T_K:T_PZ] = cols(w, n_q, 2)
        c0 = n_q + 2 * n_kv
        o[T_PZ:T_GU] = cols(w, c0, GROUPS)
        o[T_GU:T_GV] = cols(w, c0 + GROUPS * P, GROUPS)
        c0 += 2 * GROUPS * P
        o[T_GV:T_MIX] = w[:, c0:c0 + GROUPS * P].reshape(2, 4, P, 2, S).transpose(3, 0, 2, 1, 4).reshape(4, P, TILE)
        c0 += GROUPS * P
        branch = (inp["w_branch_a"][l][order], inp["w_branch_b"][l], inp["w_branch_c"][l])
        for hf in range(2):
            for br in range(BR):
                t0 = T_MIX + hf * MIX_HALF + br * 6
                o[t0:t0 + 4] = cols(w, c0 + br * D + hf * HALF_N, 4)
                wb = branch[br][:, hf * HALF_N:(hf + 1) * HALF_N]
                o[t0 + 4:t0 + 6] = wb.reshape(4, P, 2, S).transpose(2, 1, 0, 3).reshape(2, P, TILE)
        o[T_WO:T_WQ] = inp["w_out"][l].reshape(4, 2, P, 2, HALF_N).transpose(3, 0, 2, 1, 4).reshape(8, P, TILE)
        o[T_WQ:T_PU] = cols(inp["peer_w_query"][l], 0, 2 * PH)
        u = inp["peer_expert_u"][l].reshape(NK, NK, KD, P)
        v = inp["peer_expert_v"][l].reshape(NK, NK, D)
        u = u.transpose(1, 3, 2, 0).reshape(NK, P, TILE)
        v = v.transpose(1, 0, 2)
        o[T_PU:T_PV] = u[:PARKED]
        o[T_PV:T_MU] = v[:PARKED]
        o[T_MU] = u[PARKED]
        o[T_MU + 1:NT - 1:2] = u[PARKED + 1:]
        o[T_MU + 2:NT - 1:2] = v[PARKED:-1]
        o[NT - 1] = v[-1]
    return out.reshape(DEPTH * NT, P, TILE)


def kernel(**inputs):
    import concourse.bacc as bacc
    from concourse.bass_utils import run_bass_kernel_spmd

    inp = {k: np.ascontiguousarray(a) for k, a in inputs.items()}
    arrays = {
        "x": inp["x"],
        "stream": lay_out(inp),
        "consts": shape_constants(),
        "rel_bias": inp["rel_bias"],
        "final_gain": np.ascontiguousarray(np.broadcast_to(inp["final_gain"][None], (P, D))),
    }
    nc = bacc.Bacc("TRN2", target_bir_lowering=False, num_devices=1)
    args = [nc.dram_tensor(f"in_{n}", a.shape, mybir.dt.from_np(a.dtype), kind="ExternalInput").ap()
            for n, a in arrays.items()]
    out = nc.dram_tensor("out_y", (1, S, D), F32, kind="ExternalOutput").ap()
    program(nc, *args, out)
    r = run_bass_kernel_spmd(nc, [{f"in_{n}": a for n, a in arrays.items()}], core_ids=[0])
    return r.results[0]["out_y"]
```

```python
from contextlib import ExitStack

import numpy as np
import concourse.bass as bass
from concourse import mybir

F32 = mybir.dt.float32
F32R = mybir.dt.float32r
U32 = mybir.dt.uint32
ALU = mybir.AluOpType
ACT = mybir.ActivationFunctionType
AX = mybir.AxisListType

P = 128
D = 1024
KD = D // P
S = 256
TT = S // P
DEPTH = 2
HEADS, HD = 8, 64
QC = HEADS * HD // P
WINDOW = 128
BUCKETS, MAX_DIST = 32, 128
GROUPS = 4
POOL_WINDOWS = (2, 4, 8, 16)
PAD = 16
BR = 3
PH, TOPK, NK = 8, 16, 128
HALF_N = 512
EPS = 1e-6
NEG = -1e30
LOW = -3e38

TILE = 1024
RING = 4
STEPS = 4
BODY = 32
T_PARAM = 0
T_Q = T_PARAM + 2
T_K = T_Q + QC
T_V = T_K + 1
T_PZ = T_V + 1
T_GU = T_PZ + GROUPS
T_GV = T_GU + GROUPS
T_MIX = T_GV + 4
MIX_HALF = BR * 6
T_WO = T_MIX + 2 * MIX_HALF
T_WQ = T_WO + 8
T_EU = T_WQ + 2 * PH
AT_SEARCH = 40
AT_TABLE = 16
EARLY = AT_SEARCH + AT_TABLE
MAIN = NK - EARLY
T_TU = T_EU + AT_SEARCH
T_EV = T_TU + AT_TABLE
T_MU = T_EV + EARLY
NT = T_EU + 2 * NK
assert T_EU % RING == 0 and AT_SEARCH % RING == 0 and EARLY % RING == 0 and NK % RING == 0 and RING == 4
PER = BODY // KD
assert AT_TABLE * KD == S // 2 and BODY % KD == 0 and PER == RING
HIS = NT - 2 - AT_TABLE
LOP = T_EV + MAIN
TERMS = ((0, 0), (0, 1), (1, 0))

C_SK = 0
C_WPOOL = C_SK + 2 * NK
C_WSP = C_WPOOL + GROUPS * P
C_AGAIN = C_WSP + GROUPS * P
C_FGAIN = C_AGAIN + KD
C_BGATE = C_FGAIN + KD
C_PSCALE = C_BGATE + BR * KD
C_VGAIN = C_PSCALE + GROUPS
C_SINK = C_VGAIN + GROUPS
C_BSP = C_SINK + HEADS
C_END = C_BSP + GROUPS * P
assert C_END <= 2 * TILE

K_ID = 0
K_IOTA = K_ID + P
K_CINV = K_IOTA + P
K_TRIL = K_CINV + GROUPS * S
K_OH = K_TRIL + P
NDIST = 2 * P + P - 1
K_END = K_OH + NDIST

PLAN = (
    [("h1T", "V")] * 4 + [("q", "A")] * 2 + [("kv", "A")] + [("lg0", "V")] * 2 + [("lg1", "V")] * 4
    + [("pz", "V")] * 2 + [("gu", "A")] * 2 + [("pT0", "A")] * 2 + [("pT1", "A")] * 4 + [("pool", "V")] * 2
    + [("gv", "A")] * 2 + [("attn", "A")] * 4 + [("gmlp", "V")] * 2
    + ([("gate", "A")] * 2 + [("branch", "V")] * 2) * (2 * BR)
    + [("wo", "V")] * 4 + [("h2T", "V")] * 4 + [("qq", "A")] * 8 + [("score", "A")] * 8 + [("sel", "A")] * 2
)
NG = len(PLAN)
NBANK = 8
NGV = sum(who == "V" for _, who in PLAN)
NGA = NG - NGV
NCHAIN = 59
NSCAL = 14


def taken_before(group):
    return (sum(who == "V" for _, who in PLAN[:group]), sum(who == "A" for _, who in PLAN[:group]))


def bank_of(group):
    late = first("h2T")
    return group % NBANK if group < late else 4 + (group - late) % 4


def last_in_bank(group):
    if group >= first("h2T"):
        return group - 4 if group - 4 >= first("h2T") else None
    return group - NBANK if group >= NBANK else None


def first(name):
    return [n for n, _ in PLAN].index(name)


def program(nc, x_in, stream, consts_in, rel_in, fgain_in, out):
    ctx = ExitStack()
    with ctx:
        def sb(name, shape, dt=F32):
            return ctx.enter_context(nc.sbuf_tensor(name, shape, dt))

        def sem(name):
            return ctx.enter_context(nc.semaphore(name))

        area_base = -(-nc.sbuf_base // 32) * 32
        area = sb("area", [P, S * NK])
        assert nc.sbuf_base == area_base + 4 * S * NK
        ring = sb("ring", [P, RING, TILE])
        halves = sb("halves", [P, RING, 2, TILE], F32R)
        x = sb("x", [P, TT, D])
        hT = sb("hT", [P, 2, KD, S], F32R)
        act = sb("act", [P, 2, S])
        coef_base = -(-nc.sbuf_base // 32) * 32
        coef = sb("coef", [P, 2, 2, S], F32R)
        assert nc.sbuf_base == coef_base + 4 * 2 * 2 * S
        ids = sb("ids", [P, 2 * P])
        stat = sb("stat", [P, 16])
        used = [0]

        def part(*shape, dt=F32, at=None):
            n = int(np.prod(shape))
            a = used[0] if at is None else at
            if at is None:
                used[0] += n
            v = area[:, a:a + n]
            if dt != F32:
                v = v.bitcast(dt)
            if len(shape) == 1:
                return v
            names = [f"a{i}" for i in range(len(shape))]
            return v.rearrange(f"p ({' '.join(names)}) -> p {' '.join(names)}", **dict(zip(names[1:], shape[1:])))

        def halves_part(name, *shape):
            a = used[0]
            used[0] = a + 2 * int(np.prod(shape))
            return nc.alloc_sbuf_tensor_at(name, [P, 2, *shape], F32R, offset=area_base + 4 * a)

        gates_t = area[:, :].rearrange("p (e t) -> p e t", t=S)
        par = part(2 * TILE)
        bias_at = used[0]
        bias = part(HEADS, 2 * P)
        maps = part(GROUPS * S + P)
        mixed_h = [halves_part(f"{n}_halves", 4, S) for n in ("attn", "pool", "gmlp")]
        turned = part(4, 4, P, at=used[0])
        merged_h = halves_part("merged_halves", KD, S)
        hn_at = used[0]
        hn = part(TT, D)
        lg1 = part(HEADS, 2 * P, at=hn_at)
        qT_at = used[0]
        qT = part(QC, S)
        kT = part(S)
        v_tok = part(TT, P)
        lg0 = part(HEADS, P)
        pT0 = part(HEADS, P)
        pT1 = part(HEADS * 2, P, at=bias_at)
        attnT = part(QC, S, at=qT_at)
        zp = part(GROUPS, PAD + S)
        pooled_at = used[0]
        win = [part(GROUPS, PAD + S) for _ in POOL_WINDOWS]
        dT = part(GROUPS, S)
        poolT = part(GROUPS, S)
        uT = part(GROUPS, S)
        gv = part(TT, GROUPS * P)
        gmT = part(GROUPS, S)
        wsp = part(GROUPS, P)
        sig = part(2, 4, S, at=pooled_at)
        mergedT = part(KD, S, at=pooled_at + 2 * 4 * S)
        small = part(64)
        diag = part(TT, P)
        used_mix = used[0]
        used[0] = 2 * TILE
        qqT = part(PH, 2, S)
        row = part(TT, PH, 2, NK)
        val = part(TT, PH, 2, TOPK)
        idx = part(TT, PH, 2, TOPK, dt=U32)
        idf = part(TT, PH, 2, TOPK)
        cand = part(TT, PH, TOPK, TOPK)
        top = part(TT, PH, TOPK)
        ci = part(TT, PH, TOPK, dt=U32)
        ca = part(TT, PH, TOPK, dt=U32)
        cb = part(TT, PH, TOPK, dt=U32)
        caf = part(TT, PH, TOPK)
        cbf = part(TT, PH, TOPK)
        eq = part(PH, TOPK, TOPK)
        sel = part(3, TT, P)
        used[0] = max(used[0], used_mix)
        assert used[0] <= S * NK, used[0]
        x_row = x[:, :, :].rearrange("p t d -> p (t d)")
        selT = x_row[:, 0:3 * S].rearrange("p (c t) -> p c t", c=3)
        onehot1 = x_row[:, 3 * S:7 * S].rearrange("p (s u k) -> p s u k", s=STEPS, u=2)
        onehot2 = nc.alloc_sbuf_tensor_at("onehot2", [P, STEPS, 2, NK], F32, offset=coef_base)

        bank = [ctx.enter_context(nc.psum_tensor(f"bank{i}", [P, HALF_N], F32)) for i in range(NBANK)]
        acc = bank[0:4]
        bank_g = bank[4:6]
        bank_u = bank[6:8]
        act_row = act[:, :, :].rearrange("p s t -> p (s t)")
        relx = act_row[0:BUCKETS + 1, 0:HEADS]
        relv = act_row[0:HEADS, HEADS:HEADS + NDIST]
        oh = area[0:BUCKETS + 1, S * NK - NDIST:S * NK]
        scratch = nc.dram_tensor("rel_scratch", (HEADS, P, NDIST), F32).ap()
        early_dram = nc.dram_tensor("early_blocks", (EARLY, P, S), F32).ap()

        ident = ids[:, K_ID:K_ID + P]
        iota = ids[:, K_IOTA:K_IOTA + P]
        cinv = maps[:, 0:GROUPS * S].rearrange("p (g t) -> p g t", g=GROUPS)
        tril = maps[:, GROUPS * S:]

        loaded = [sem(f"loaded{i}") for i in range(RING)]
        tiles_used = sem("tiles_used")
        x_loaded = sem("x_loaded")
        consts_loaded = sem("consts_loaded")
        rel_loaded = sem("rel_loaded")
        rel_low = sem("rel_low")
        rel_product = sem("rel_product")
        rel_vector = sem("rel_vector")
        rel_written = sem("rel_written")
        bias_loaded = sem("bias_loaded")
        maps_loaded = sem("maps_loaded")
        params_ready = sem("params_ready")
        hi_done = sem("hi_done")
        lo_pool = sem("lo_pool")
        lo_vector = sem("lo_vector")
        mixed_ready = sem("mixed_ready")
        scaled = sem("scaled")
        wsp_ready = sem("wsp_ready")
        root_ready = sem("root_ready")
        rstd_ready = sem("rstd_ready")
        diag_ready = sem("diag_ready")
        hi_rows = sem("hi_rows")
        groups_done = sem("groups_done")
        taken_v = sem("taken_v")
        taken_a = sem("taken_a")
        chain = sem("chain")
        scal = sem("scal")
        max_ready = sem("max_ready")
        exp_ready = sem("exp_ready")
        probs_ready = sem("probs_ready")
        diff_ready = sem("diff_ready")
        vhat_ready = sem("vhat_ready")
        merged_ready = sem("merged_ready")
        shifted_ready = sem("shifted_ready")
        gexp_ready = sem("gexp_ready")
        sel_ready = sem("sel_ready")
        square_done = sem("square_done")
        onehot_ready = sem("onehot_ready")
        onehots_ready = sem("onehots_ready")
        outer_done = sem("outer_done")
        table_ready = sem("table_ready")
        act_done = sem("act_done")
        hi_pool = sem("hi_pool")
        early_stored = [sem(f"early_stored{i}") for i in range(2)]
        early_loaded = [sem(f"early_loaded{i}") for i in range(2)]
        product_ready = sem("product_ready")
        coef_hi = sem("coef_hi")
        coef_ready = sem("coef_ready")
        x_ready = sem("x_ready")
        fgain_loaded = sem("fgain_loaded")
        out_ready = sem("out_ready")
        out_written = sem("out_written")

        NQ = S // 2
        NG4 = S // 4

        block = ctx.enter_context(nc.Block())

        @block.sync
        def _(sp):
            sp.dma_start(x[:, :, :], x_in.rearrange("b (t p) d -> p (b t) d", p=P)).then_inc(x_loaded, 16)
            sp.dma_start(ids[:, :], consts_in[:, 0:2 * P]).then_inc(consts_loaded, 16)
            sp.dma_start(oh, consts_in[0:BUCKETS + 1, K_OH:K_END]).then_inc(rel_loaded, 16)
            sp.dma_start(relx[0:BUCKETS, :], rel_in).then_inc(rel_loaded, 16)

            def load(n, s, l):
                sp.dma_start(ring[:, s, :], stream[bass.ds(l * NT + n, 1)].rearrange("a p c -> (a p) c"))\
                    .then_inc(loaded[s], 16)

            for k in range(2):
                sp.sem_inc(early_stored[k], 16)

            with sp.Fori(0, DEPTH) as l:
                sp.wait_ge(lo_pool, l * LOP + 1)
                sp.wait_ge(lo_vector, l * NK + 1)
                for s in range(RING):
                    load(s, s, l)
                sp.wait_ge(params_ready, l + 1)
                sp.dma_start(maps, consts_in[:, K_CINV:K_OH]).then_inc(maps_loaded, 16)
                for s in range(RING):
                    sp.wait_ge(lo_pool, l * LOP + (s + 2))
                    load(RING + s, s, l)
                sp.wait_ge(rel_written, 16)
                sp.dma_start(bias, bass.AP(scratch.tensor, P - 1, [[NDIST - 1, P], [P * NDIST, HEADS], [1, 2 * P]]))\
                    .then_inc(bias_loaded, 16)
                with sp.Fori(2, T_EU // RING + 1) as r:
                    for s in range(RING):
                        sp.wait_ge(lo_pool, l * LOP + r * RING + (s - RING + 2))
                        load(r * RING + s, s, l)

                def store(b, k):
                    sp.wait_ge(act_done, l * NK + b + 1)
                    sp.dma_start(early_dram[bass.ds(b, 1)].rearrange("a p t -> (a p) t"), act[:, k, :])\
                        .then_inc(early_stored[k], 16)

                def load_behind(r, s):
                    sp.wait_ge(lo_pool, l * LOP + r * RING + (T_EU + s + 2))
                    load(r * RING + (T_EU + RING + s), s, l)

                for s in range(RING):
                    load_behind(0, s)
                    if s >= 2:
                        store(s - 2, s % 2)
                with sp.Fori(1, EARLY // RING) as r:
                    for s in range(RING):
                        load_behind(r, s)
                        store(r * RING + (s - 2), s % 2)
                def reload(b, k):
                    sp.dma_start(act[:, k, :], early_dram[bass.ds(b, 1)].rearrange("a p t -> (a p) t"))\
                        .then_inc(early_loaded[k], 16)

                def load_v(r, s, more):
                    sp.wait_ge(lo_vector, l * NK + r * RING + (s + 2))
                    load(r * RING + (T_EV + RING + s), s, l)
                    if more:
                        sp.wait_ge(coef_ready, l * NK + r * RING + (s + 1))
                        reload(r * RING + s, s % 2)

                with sp.Fori(0, EARLY // RING - 1) as r:
                    for s in range(RING):
                        load_v(r, s, True)
                for s in range(RING):
                    load_v(EARLY // RING - 1, s, s < 2)
                for s in range(RING):
                    if s in (0, 1, 3):
                        sp.wait_ge(lo_pool, l * LOP + (T_EV + 1 + (1, 2, 0, 3)[s]))
                    else:
                        sp.wait_ge(lo_vector, l * NK + (EARLY + 2))
                    load(T_MU + RING + s, s, l)
                with sp.Fori(2, 2 * MAIN // RING) as r:
                    for s in range(RING):
                        if s % 2:
                            sp.wait_ge(lo_pool, l * LOP + r * 2 + (T_EV + 1 + (s - 1) // 2))
                        else:
                            sp.wait_ge(lo_vector, l * NK + r * 2 + (EARLY - 1 + s // 2))
                        load(r * RING + (T_MU + s), s, l)
            sp.wait_ge(x_ready, 4 * DEPTH + 4)
            sp.dma_start(ring[:, 0, :], fgain_in).then_inc(fgain_loaded, 16)
            for t in range(TT):
                sp.wait_ge(out_ready, t + 1)
                sp.dma_start(out.rearrange("b (t p) d -> p (b t) d", p=P)[:, t, :], x[:, t, :]).then_inc(out_written, 16)
            sp.wait_ge(out_written, 16 * TT)

        @block.gpsimd
        def _(pool):
            pool.memset(relx[BUCKETS:BUCKETS + 1, :], NEG).then_inc(rel_low, 1)
            pool.wait_ge(rel_low, 1)
            pool.sem_inc(lo_pool, 1)
            pool.wait_ge(rel_vector, 1)
            pool.wait_ge(loaded[RING - 1], 16)
            pool.dma_start(scratch, relv.unsqueeze(1).to_broadcast([HEADS, P, NDIST])).then_inc(rel_written, 16)
            pool.wait_ge(consts_loaded, 16)

            def subtract(s):
                pool.tensor_tensor(halves[:, s, 1, :], ring[:, s, :], halves[:, s, 0, :].bitcast(F32), ALU.subtract)\
                    .then_inc(lo_pool, 1)

            def low(n, s, l, before=0):
                pool.wait_ge(hi_done, l * HIS + n - (before + 1))
                subtract(s)

            with pool.Fori(0, DEPTH) as l:
                pool.wait_ge(params_ready, l + 1)
                pool.sem_inc(lo_pool, 2)
                low(2, 2, l)
                low(3, 3, l)
                pool.wait_ge(maps_loaded, l * 16 + 16)
                for g in range(GROUPS):
                    i = pool.tensor_tensor(wsp[:, g, :], par[:, C_WSP + g * P:C_WSP + (g + 1) * P], tril, ALU.mult)
                i.then_inc(wsp_ready, 1)
                with pool.Fori(1, T_TU // RING) as r:
                    for s in range(RING):
                        low(r * RING + s, s, l)
                with pool.Fori(0, AT_TABLE // RING) as r:
                    for s in range(RING):
                        n = r * RING + (T_TU + s)
                        pool.wait_ge(tiles_used, l * NT + n - (RING - 1))
                        pool.wait_ge(loaded[s], l * (16 * NT // RING) + (n - s) * (16 // RING) + 16)
                        pool.tensor_tensor(halves[:, s, 0, :], ring[:, s, :], stat[:, 12:13].to_broadcast([P, TILE]),
                                           ALU.mult).then_inc(hi_pool, 1)
                        pool.wait_ge(hi_pool, l * AT_TABLE + r * RING + (s + 1))
                        subtract(s)
                low(T_MU, 0, l, AT_TABLE)
                with pool.Fori(0, (MAIN - 1) // 2) as r:
                    low(r * 4 + (T_MU + 1), 1, l, AT_TABLE)
                    low(r * 4 + (T_MU + 3), 3, l, AT_TABLE)
                low(NT - 3, 1, l, AT_TABLE)

        @block.scalar
        def _(a):
            eps = stat[:, 15:16]
            one = stat[:, 12:13]

            def roots(base, wait):
                def squares(i):
                    wait(i)
                    hf, t = divmod(i, TT)
                    h = slice(hf * HALF_N, (hf + 1) * HALF_N)
                    a.activation(hn[:, t, h], x[:, t, h], ACT.Square, accum_out=stat[:, 6 * hf + t:6 * hf + t + 1])\
                        .then_inc(scal, 1)

                a.activation(stat[:, 13:14], one, ACT.Sqrt)
                for i in range(3):
                    squares(i)
                a.wait_ge(scal, base + 3)
                a.activation(stat[:, 0:2], stat[:, 0:2], ACT.Identity, bias=eps, scale=1.0 / D).then_inc(scal, 1)
                squares(3)
                a.wait_ge(scal, base + 5)
                for t in range(TT):
                    i = a.activation(stat[:, 2 + t:3 + t], stat[:, 6 + t:7 + t], ACT.Sqrt, bias=stat[:, t:t + 1],
                                     scale=1.0 / D)
                i.then_inc(root_ready, 1)

            a.sem_inc(table_ready, 2)
            a.wait_ge(chain, 1)
            with a.Fori(0, DEPTH) as l:
                g = [0]
                next_tile = [2]

                def high(n, s):
                    a.wait_ge(loaded[s], l * (16 * NT // RING) + (n - s) * (16 // RING) + 16)
                    a.activation(halves[:, s, 0, :], ring[:, s, :], ACT.Copy).then_inc(hi_done, 1)

                def high_up_to(last):
                    while next_tile[0] <= last:
                        n = next_tile[0]
                        if n >= RING:
                            a.wait_ge(tiles_used, l * NT + (n - RING + 1))
                        high(n, n % RING)
                        next_tile[0] += 1

                def group(name):
                    while PLAN[g[0]][1] != "A":
                        g[0] += 1
                    assert PLAN[g[0]][0] == name, (PLAN[g[0]], name)
                    a.wait_ge(groups_done, l * NG + (g[0] + 1))
                    g[0] += 1
                    return bank[bank_of(g[0] - 1)]

                def high_rows(name):
                    for c in range(4):
                        n, t = divmod(c, TT)
                        a.wait_ge(taken_v, l * NGV + taken_before(first(name) + c + 1)[0])
                        a.activation(hT[:, 0, 4 * n:4 * n + 4, t * P:(t + 1) * P], turned[:, c], ACT.Copy)\
                            .then_inc(hi_rows, 1)

                roots(l * NSCAL, lambda i: a.wait_ge(x_ready, l * 4 + (i + 1)))
                for n in range(2):
                    a.wait_ge(loaded[n], l * (16 * NT // RING) + 16)
                    a.activation(par[:, n * TILE:(n + 1) * TILE], ring[:, n, :], ACT.Copy).then_inc(scal, 1)
                a.wait_ge(scal, l * NSCAL + 7)
                a.sem_inc(params_ready, 1)
                high_up_to(RING - 1)
                high_rows("h1T")
                for n in range(2):
                    high_up_to(T_Q + 2 * n + 1 + 3)
                    b = group("q")
                    a.activation(qT[:, 2 * n:2 * n + 2, :], b[:, :].rearrange("p (c t) -> p c t", c=2), ACT.Copy)\
                        .then_inc(taken_a, 1)
                high_up_to(T_V + 3)
                b = group("kv")
                a.activation(kT, b[:, 0:S], ACT.Copy)
                a.activation(v_tok, b[:, S:].rearrange("p (t c) -> p t c", t=TT), ACT.Copy).then_inc(taken_a, 1)
                for blk, lg in ((0, lg0), (1, lg1)):
                    high_up_to(T_GU + 2 * blk)
                    a.wait_ge(max_ready, l * 2 + (blk + 1))
                    for h in range(HEADS):
                        a.activation(lg[:, h, :], lg[:, h, :], ACT.Exp, bias=small[:, blk * 32 + h:blk * 32 + h + 1],
                                     accum_out=small[:, blk * 32 + 16 + h:blk * 32 + 17 + h])
                    a.activation(small[:, blk * 32 + 24:blk * 32 + 32], small[:, blk * 32 + 8:blk * 32 + 16], ACT.Exp)\
                        .then_inc(exp_ready, 1)
                for n in range(2):
                    high_up_to(T_GU + 2 * n + 1 + 3)
                    b = group("gu")
                    a.activation(uT[:, 2 * n:2 * n + 2, :], b[:, :].rearrange("p (c t) -> p c t", c=2),
                                 ACT.Gelu_apprx_tanh).then_inc(taken_a, 1)
                for n in range(2):
                    b = group("pT0")
                    a.activation(pT0[:, 4 * n:4 * n + 4, :], b[:, :].rearrange("p (c t) -> p c t", c=4), ACT.Copy)\
                        .then_inc(taken_a, 1)
                for n in range(4):
                    b = group("pT1")
                    a.activation(pT1[:, 4 * n:4 * n + 4, :], b[:, :].rearrange("p (c t) -> p c t", c=4), ACT.Copy)\
                        .then_inc(taken_a, 1)
                for t in range(TT):
                    high_up_to(T_GV + 3 + 3)
                    b = group("gv")
                    a.activation(gv[:, t, :], b[:, :], ACT.Gelu_apprx_tanh).then_inc(taken_a, 1)
                a.wait_ge(taken_a, l * NGA + taken_before(first("attn"))[1])
                for t in range(TT):
                    a.activation(attnT[:, 2 * t:2 * t + 2, :], gv[:, t, :].rearrange("p (c t) -> p c t", c=2),
                                 ACT.Square, accum_out=stat[:, 6 + t:7 + t])\
                        .then_inc(scal, 1)
                a.wait_ge(scal, l * NSCAL + 9)
                a.activation(stat[:, 8:10], stat[:, 6:8], ACT.Sqrt, bias=eps, scale=1.0 / (GROUPS * P))\
                    .then_inc(root_ready, 1)
                for c in range(QC):
                    b = group("attn")
                    a.activation(attnT[0:HD, c, :], b[0:HD, 0:S], ACT.Copy)
                    a.activation(attnT[HD:P, c, :], b[HD:P, S:], ACT.Copy).then_inc(taken_a, 1)
                for hf in range(2):
                    for br in range(BR):
                        if 3 * hf + br >= 2:
                            a.wait_ge(taken_v, l * NGV + taken_before(first("gate") + 4 * (3 * hf + br - 1))[0])
                        for n in range(2):
                            high_up_to(T_MIX + 6 * (3 * hf + br) + 2 * n + 1 + 3)
                            b = group("gate")
                            for c in range(2):
                                col = C_BGATE + br * KD + hf * 4 + 2 * n + c
                                i = a.activation(sig[:, (3 * hf + br) % 2, 2 * n + c, :], b[:, c * S:(c + 1) * S],
                                                 ACT.Sigmoid, bias=par[:, col:col + 1])
                            i.then_inc(taken_a, 1)
                high_up_to(T_WO + 7 + 3)
                roots(l * NSCAL + 9, lambda i: a.wait_ge(taken_v, l * NGV + taken_before(first("wo") + i + 1)[0]))
                high_rows("h2T")
                for h in range(PH):
                    high_up_to(T_WQ + 2 * h + 1 + 3)
                    b = group("qq")
                    a.activation(qqT[:, h], b[:, :].rearrange("p (c t) -> p c t", c=2), ACT.Copy).then_inc(taken_a, 1)
                for n in range(8):
                    b = group("score")
                    a.activation(row[:, n // 4, 2 * (n % 4):2 * (n % 4) + 2].rearrange("p h c k -> p (h c k)"),
                                 b[:, :], ACT.Copy).then_inc(taken_a, 1)
                def gelu(k):
                    a.activation(act[:, k, :], bank_u[k][:, 0:S], ACT.Gelu_apprx_tanh).then_inc(act_done, 1)

                def park(r, s):
                    a.wait_ge(tiles_used, l * NT + r * RING + (T_EU + s + 1))
                    a.wait_ge(early_stored[s % 2], l * (8 * (EARLY - 2)) + r * (8 * RING) + 16 * (s // 2 + 1))
                    gelu(s % 2)

                high_up_to(T_EU + RING - 1)
                a.activation(stat[:, 13:14], one, ACT.Gelu_apprx_tanh)
                with a.Fori(0, AT_SEARCH // RING - 1) as r:
                    for s in range(RING):
                        a.wait_ge(tiles_used, l * NT + r * RING + (T_EU + s + 1))
                        high(r * RING + (T_EU + RING + s), s)
                        park(r, s)
                a.wait_ge(shifted_ready, l + 1)
                a.activation(sel[:, 2], sel[:, 2], ACT.Exp).then_inc(gexp_ready, 1)
                for s in range(RING):
                    if s == RING - 1:
                        for t in range(TT):
                            b = group("sel")
                            a.activation(selT[:, :, t * P:(t + 1) * P], b[:, 0:3 * P].rearrange("p (c t) -> p c t", c=3),
                                         ACT.Copy).then_inc(taken_a, 1)
                    park(AT_SEARCH // RING - 1, s)
                a.wait_ge(taken_a, l * NGA + NGA)
                with a.Fori(0, NQ // BODY) as j:
                    def onehot(q):
                        a.wait_ge(outer_done, l * NQ + j * BODY + (q + 1))
                        rows = onehot1[:, q % STEPS, 1, :]
                        a.activation(rows, iota, ACT.Square,
                                     bias=selT[:, 0, bass.ds(j * (2 * BODY) + (2 * q + 1), 1)], scale=-1.0)\
                            .then_inc(square_done, 1)
                        a.wait_ge(square_done, l * NG4 + j * (BODY // 2) + (q // 2 + 1))
                        a.activation(rows, rows, ACT.Relu, bias=one, scale=-4.0).then_inc(onehot_ready, 1)

                    def table(g4):
                        a.wait_ge(outer_done, l * NQ + j * BODY + (STEPS + 2 * (g4 + 1)))
                        a.activation(gates_t[:, :, bass.ds(j * (2 * BODY) + 4 * g4, 4)],
                                     bank_g[g4 % 2][:, :].rearrange("p (t e) -> p e t", t=4), ACT.Copy)\
                            .then_inc(table_ready, 1)

                    def hold(i):
                        a.wait_ge(tiles_used, l * NT + j * PER + (T_TU + i + 1))
                        a.wait_ge(early_stored[i % 2], l * (8 * (EARLY - 2)) + j * (8 * PER) + (8 * AT_SEARCH + 16 * (i // 2 + 1)))
                        gelu(i % 2)

                    for q in range(BODY):
                        if q % 2 == 0 and q >= 4:
                            table(q // 2 - 2)
                        if q % 2:
                            onehot(q)
                        if q % KD == 3 and q > KD:
                            hold(q // KD - 1)
                    table(BODY // 2 - 2)
                    table(BODY // 2 - 1)
                    hold(PER - 1)
                for s in range(RING):
                    a.wait_ge(tiles_used, l * NT + (T_EV - RING + s + 1))
                    high(T_EV + s, s)
                with a.Fori(0, EARLY // RING) as r:
                    for s in range(RING):
                        a.wait_ge(tiles_used, l * NT + r * RING + (T_EV + s + 1))
                        high(r * RING + (T_EV + RING + s), s)

                def main(p, s, block=None, last=False):
                    a.wait_ge(tiles_used, l * NT + p + (T_MU + 1))
                    if not last:
                        high(p + (T_MU + RING), s)
                    if block is not None:
                        k = 1 if s == 1 else 0
                        a.wait_ge(coef_ready, l * NK + block - 1)
                        gelu(k)

                main(0, 0, EARLY)
                with a.Fori(0, MAIN // 2 - 2) as r:
                    main(r * 4 + 1, 1, r * 2 + (EARLY + 1))
                    main(r * 4 + 2, 2)
                    main(r * 4 + 3, 3, r * 2 + (EARLY + 2))
                    main(r * 4 + 4, 0)
                end = 2 * MAIN - 7
                main(end, 1, NK - 3)
                main(end + 1, 2)
                main(end + 2, 3, NK - 2)
                main(end + 4, 1, NK - 1, last=True)
            roots(NSCAL * DEPTH, lambda i: a.wait_ge(x_ready, 4 * DEPTH + (i + 1)))

        @block.vector
        def _(v):
            v.memset(stat[:, 12:13], 1.0)
            v.memset(stat[:, 15:16], EPS).then_inc(chain, 1)
            v.sem_inc(lo_vector, 1)
            v.wait_ge(x_loaded, 16)
            v.sem_inc(x_ready, 4)
            v.wait_ge(rel_product, 1)
            v.tensor_copy(relv, bank[0][0:HEADS, 0:NDIST]).then_inc(rel_vector, 1)

            with v.Fori(0, DEPTH) as l:
                links = [1]

                def link(ins):
                    links[0] += 1
                    ins.then_inc(chain, 1)
                    v.wait_ge(chain, l * NCHAIN + links[0])

                g = [0]

                def group(name):
                    while PLAN[g[0]][1] != "V":
                        g[0] += 1
                    assert PLAN[g[0]][0] == name, (PLAN[g[0]], name)
                    v.wait_ge(groups_done, l * NG + (g[0] + 1))
                    g[0] += 1
                    return bank[bank_of(g[0] - 1)]

                def halve(halves, full):
                    link(v.tensor_copy(halves[0], full))
                    return v.tensor_tensor(halves[1], full, halves[0].bitcast(F32), ALU.subtract)

                def transposed(name, col):
                    for n in range(2):
                        for t in range(TT):
                            b = group(name)
                            i = v.tensor_tensor(
                                turned[:, 2 * n + t], b[:, :].rearrange("p (k t) -> p k t", k=4),
                                par[:, col + 4 * n:col + 4 * n + 4].unsqueeze(2).to_broadcast([P, 4, P]), ALU.mult)
                            i.then_inc(taken_v, 1)
                        for t in range(TT):
                            v.wait_ge(hi_rows, l * 8 + (0 if name == "h1T" else 4) + 2 * n + t + 1)
                            hi, lo = (hT[:, c, 4 * n:4 * n + 4, t * P:(t + 1) * P] for c in range(2))
                            i = v.tensor_tensor(lo, turned[:, 2 * n + t], hi.bitcast(F32), ALU.subtract)
                        i.then_inc(scaled, 1)

                def rstd(n, at, to):
                    v.wait_ge(root_ready, l * 3 + n)
                    v.reciprocal(stat[:, to:to + 2], stat[:, at:at + 2]).then_inc(rstd_ready, 1)
                    v.wait_ge(rstd_ready, l * 3 + n)

                def diagonals():
                    for t in range(TT):
                        i = v.tensor_scalar(diag[:, t, :], ident, stat[:, 4 + t:5 + t], None, ALU.mult)
                    i.then_inc(diag_ready, 1)

                rstd(1, 2, 4)
                diagonals()
                v.wait_ge(params_ready, l + 1)
                transposed("h1T", C_AGAIN)
                v.wait_ge(bias_loaded, l * 16 + 16)
                for blk, lg, per in ((0, lg0, 4), (1, lg1, 2)):
                    for n in range(HEADS // per):
                        b = group(f"lg{blk}")
                        i = v.scalar_tensor_tensor(
                            lg[:, per * n:per * n + per, :], b[:, :].rearrange("p (h s) -> p h s", h=per), HD ** -0.5,
                            bias[:, per * n:per * n + per, (1 - blk) * P:], ALU.mult, ALU.add)
                        i.then_inc(taken_v, 1)
                    v.wait_ge(taken_v, l * NGV + (6 if blk == 0 else 10))
                    o = blk * 32
                    link(v.tensor_reduce(small[:, o:o + 8], lg, AX.X, ALU.max))
                    link(v.tensor_tensor(small[:, o:o + 8], small[:, o:o + 8], par[:, C_SINK:C_SINK + 8], ALU.max))
                    link(v.tensor_scalar(small[:, o:o + 8], small[:, o:o + 8], -1.0, None, ALU.mult))
                    v.tensor_tensor(small[:, o + 8:o + 16], small[:, o:o + 8], par[:, C_SINK:C_SINK + 8], ALU.add)\
                        .then_inc(max_ready, 1)
                v.wait_ge(maps_loaded, l * 16 + 16)
                link(v.memset(zp[:, :, 0:PAD], 0.0))
                for n in range(2):
                    b = group("pz")
                    v.tensor_copy(zp[:, 2 * n:2 * n + 2, PAD:], b[:, :].rearrange("p (c t) -> p c t", c=2))\
                        .then_inc(taken_v, 1)
                v.wait_ge(taken_v, l * NGV + 12)
                src = zp
                for n, w in enumerate(POOL_WINDOWS):
                    link(v.tensor_tensor(win[n][:, n:, w - 1:], src[:, n:, w - 1:],
                                         src[:, n:, w - 1 - w // 2:PAD + S - w // 2], ALU.add))
                    src = win[n]
                for n in range(GROUPS):
                    i = v.tensor_tensor(dT[:, n, :], win[n][:, n, PAD:], cinv[:, n, :], ALU.mult)
                link(i)
                v.tensor_tensor(dT, dT, zp[:, :, PAD:], ALU.subtract).then_inc(diff_ready, 1)
                for blk, lg in ((0, lg0), (1, lg1)):
                    o = blk * 32
                    v.wait_ge(exp_ready, l * 2 + (blk + 1))
                    link(v.tensor_tensor(small[:, o + 16:o + 24], small[:, o + 16:o + 24], small[:, o + 24:o + 32], ALU.add))
                    link(v.reciprocal(small[:, o + 16:o + 24], small[:, o + 16:o + 24]))
                    v.tensor_tensor(lg, lg, small[:, o + 16:o + 24].unsqueeze(2).to_broadcast([P, HEADS, (blk + 1) * P]),
                                    ALU.mult).then_inc(probs_ready, 1)
                for n in range(2):
                    b = group("pool")
                    v.tensor_tensor(
                        poolT[:, 2 * n:2 * n + 2, :], b[:, :].rearrange("p (c t) -> p c t", c=2),
                        par[:, C_PSCALE + 2 * n:C_PSCALE + 2 * n + 2].unsqueeze(2).to_broadcast([P, 2, S]), ALU.mult,
                    ).then_inc(taken_v, 1)
                rstd(2, 8, 10)
                for t in range(TT):
                    i = v.tensor_scalar(gv[:, t, :], gv[:, t, :], stat[:, 10 + t:11 + t], None, ALU.mult)
                i.then_inc(vhat_ready, 1)
                bsp = par[:, C_BSP:C_BSP + GROUPS * P].rearrange("p (g t) -> p g t", g=GROUPS)
                for n in range(2):
                    b = group("gmlp")
                    for c in range(2):
                        i = v.scalar_tensor_tensor(
                            gmT[:, 2 * n + c, :].rearrange("p (c t) -> p c t", c=2),
                            b[:, c * S:(c + 1) * S].rearrange("p (c t) -> p c t", c=2),
                            par[:, C_VGAIN + 2 * n + c:C_VGAIN + 2 * n + c + 1],
                            bsp[:, 2 * n + c, :].unsqueeze(1).to_broadcast([P, 2, P]), ALU.mult, ALU.add)
                    i.then_inc(taken_v, 1)
                v.wait_ge(taken_v, l * NGV + 16)
                v.wait_ge(taken_a, l * NGA + 5)
                link(v.tensor_tensor(gmT, gmT, uT, ALU.mult))
                v.wait_ge(taken_a, l * NGA + taken_before(first("gate"))[1])
                for m_h, m in zip(mixed_h, (attnT, poolT, gmT)):
                    halve((m_h[:, 0], m_h[:, 1]), m).then_inc(mixed_ready, 1)
                for hf in range(2):
                    for br in range(BR):
                        for n in range(2):
                            b = group("branch")
                            y = b[:, :].rearrange("p (c t) -> p c t", c=2)
                            m = mergedT[:, 4 * hf + 2 * n:4 * hf + 2 * n + 2, :]
                            s = sig[:, (3 * hf + br) % 2, 2 * n:2 * n + 2, :]
                            v.wait_ge(taken_a, l * NGA + taken_before(g[0])[1])
                            if br == 0:
                                v.tensor_tensor(m, s, y, ALU.mult).then_inc(taken_v, 1)
                            else:
                                tmp = zp[:, 2 * n:2 * n + 2, 0:S]
                                i = v.tensor_tensor(tmp, s, y, ALU.mult)
                                i.then_inc(taken_v, 1)
                                v.wait_ge(taken_v, l * NGV + taken_before(g[0])[0])
                                link(v.tensor_tensor(m, m, tmp, ALU.add))
                            if br == BR - 1:
                                c = slice(4 * hf + 2 * n, 4 * hf + 2 * n + 2)
                                halve((merged_h[:, 0, c], merged_h[:, 1, c]), m).then_inc(merged_ready, 1)
                for hf in range(2):
                    for t in range(TT):
                        b = group("wo")
                        xs = x[:, t, hf * HALF_N:(hf + 1) * HALF_N]
                        v.tensor_tensor(xs, xs, b[:, :], ALU.add).then_inc(taken_v, 1)
                rstd(3, 2, 4)
                diagonals()
                transposed("h2T", C_FGAIN)

                def then_search(ins):
                    links[0] += 1
                    ins.then_inc(chain, 1)
                    v.wait_ge(chain, l * NCHAIN + links[0])
                    v.memset(stat[:, 14:15], 0.0)

                v.wait_ge(taken_a, l * NGA + NGA - 2)
                v.memset(stat[:, 14:15], 0.0)
                rows = [(t, h, c) for t in range(TT) for h in range(PH) for c in range(2)]
                for k in range(2):
                    for t, h, c in rows:
                        i = v.max(val[:, t, h, c, 8 * k:8 * k + 8], row[:, t, h, c, :])
                    then_search(i)
                    for t, h, c in rows:
                        i = v.max_index(idx[:, t, h, c, 8 * k:8 * k + 8], val[:, t, h, c, 8 * k:8 * k + 8], row[:, t, h, c, :])
                    then_search(i)
                    if k == 0:
                        for t, h, c in rows:
                            i = v.match_replace(row[:, t, h, c, :], val[:, t, h, c, 0:8], row[:, t, h, c, :], LOW)
                        then_search(i)
                v.tensor_copy(idf.rearrange("p a b c d -> p (a b c d)"), idx.rearrange("p a b c d -> p (a b c d)"))
                for t in range(TT):
                    i = v.tensor_tensor(cand[:, t], val[:, t, :, 0, :].unsqueeze(3).to_broadcast([P, PH, TOPK, TOPK]),
                                        val[:, t, :, 1, :].unsqueeze(2).to_broadcast([P, PH, TOPK, TOPK]), ALU.add)
                then_search(i)
                pairs = [(t, h) for t in range(TT) for h in range(PH)]
                for k in range(2):
                    ks = slice(8 * k, 8 * k + 8)
                    flat = [cand[:, t, h].rearrange("p a b -> p (a b)") for t, h in pairs]
                    for (t, h), f in zip(pairs, flat):
                        i = v.max(top[:, t, h, ks], f)
                    then_search(i)
                    for (t, h), f in zip(pairs, flat):
                        i = v.max_index(ci[:, t, h, ks], top[:, t, h, ks], f)
                    then_search(i)
                    if k == 0:
                        for (t, h), f in zip(pairs, flat):
                            i = v.match_replace(f, top[:, t, h, ks], f, LOW)
                        then_search(i)
                gate = sel[:, 2].rearrange("p t (h j) -> p t h j", h=PH)
                for t in range(TT):
                    i = v.tensor_tensor(gate[:, t], top[:, t], top[:, t, :, 0:1].to_broadcast([P, PH, TOPK]), ALU.subtract)
                i.then_inc(shifted_ready, 1)
                v.tensor_scalar(ca.rearrange("p t h j -> p (t h j)"), ci.rearrange("p t h j -> p (t h j)"), 4, None,
                                ALU.logical_shift_right)
                link(v.tensor_scalar(cb.rearrange("p t h j -> p (t h j)"), ci.rearrange("p t h j -> p (t h j)"), 15, None,
                                     ALU.bitwise_and))
                v.tensor_copy(caf, ca)
                link(v.tensor_copy(cbf, cb))
                for c, rank in ((0, caf), (1, cbf)):
                    for t in range(TT):
                        link(v.tensor_tensor(eq, rank[:, t].unsqueeze(3).to_broadcast([P, PH, TOPK, TOPK]),
                                             iota[:, 0:TOPK].unsqueeze(1).unsqueeze(1).to_broadcast([P, PH, TOPK, TOPK]),
                                             ALU.is_equal))
                        link(v.tensor_tensor(eq, eq, idf[:, t, :, c, :].unsqueeze(2).to_broadcast([P, PH, TOPK, TOPK]),
                                             ALU.mult))
                        link(v.tensor_reduce(sel[:, c, t].rearrange("p (h j) -> p h j", h=PH), eq, AX.X, ALU.add))
                v.wait_ge(gexp_ready, l + 1)
                gs = small[:, 0:16].rearrange("p (t h) -> p t h", t=TT)
                link(v.tensor_reduce(gs, gate, AX.X, ALU.add))
                link(v.reciprocal(gs, gs))
                for t in range(TT):
                    i = v.tensor_tensor(gate[:, t], gate[:, t], gs[:, t].unsqueeze(2).to_broadcast([P, PH, TOPK]), ALU.mult)
                i.then_inc(sel_ready, 1)
                with v.Fori(0, NQ // BODY) as j:
                    v.wait_ge(taken_a, l * NGA + NGA)

                    def onehots(q):
                        s = q % STEPS
                        v.wait_ge(outer_done, l * NQ + j * BODY + (q + 1))
                        for u in range(2):
                            key1, key2, weight = (selT[:, c, bass.ds(j * (2 * BODY) + (2 * q + u), 1)] for c in range(3))
                            if q % 2 == 0 or u == 0:
                                v.tensor_scalar(onehot1[:, s, u, :], iota, key1, None, ALU.is_equal)
                            i = v.tensor_scalar(onehot2[:, s, u, :], iota, key2, weight, ALU.is_equal, ALU.mult)
                        i.then_inc(onehots_ready, 1)

                    for q in range(BODY):
                        onehots(q)

                def low(b, n, s):
                    v.wait_ge(hi_done, l * HIS + n - (AT_TABLE + 1))
                    v.tensor_tensor(halves[:, s, 1, :], ring[:, s, :], halves[:, s, 0, :].bitcast(F32), ALU.subtract)\
                        .then_inc(lo_vector, 1)

                def gated(b, k, n, s, used_at, block=None, last=False):
                    low(b, n, s)
                    if block is not None and not last:
                        v.wait_ge(early_loaded[k], l * (8 * (EARLY - 2)) + (b - k) * 8)
                    else:
                        v.wait_ge(act_done, l * NK + (b if block is None else block) + 1)
                    full = act[:, k, :]
                    v.tensor_tensor(full, full, gates_t[:, bass.ds(b if block is None else block, 1), :].rearrange("p e t -> p (e t)"),
                                    ALU.mult).then_inc(product_ready, 1)
                    v.wait_ge(product_ready, l * NK + b + 1)
                    v.wait_ge(tiles_used, l * NT + used_at)
                    v.tensor_copy(coef[:, k, 0, :], full).then_inc(coef_hi, 1)
                    v.wait_ge(coef_hi, l * NK + b + 1)
                    v.tensor_tensor(coef[:, k, 1, :], full, coef[:, k, 0, :].bitcast(F32), ALU.subtract)\
                        .then_inc(coef_ready, 1)

                v.wait_ge(table_ready, l * NG4 + (NG4 + 2))
                for s in range(RING):
                    gated(s, s % 2, s + T_EV, s, s + (T_EV - 1), block=(s - 2) % EARLY, last=s < 2)
                with v.Fori(1, EARLY // RING) as r:
                    for s in range(RING):
                        b = r * RING + s
                        gated(b, s % 2, b + T_EV, s, b + (T_EV - 1), block=r * RING + (s - 2))
                gated(EARLY, 0, T_MU + 2, 2, T_MU - 1)
                gated(EARLY + 1, 1, T_MU + 4, 0, T_MU)
                with v.Fori(1, MAIN // 2 - 1) as r:
                    for k in range(2):
                        gated(r * 2 + (EARLY + k), k, r * 4 + (T_MU + 2 + 2 * k), (2, 0)[k], r * 4 + (T_MU - 1 + 2 * k))
                gated(NK - 2, 0, NT - 2, 2, NT - 5)
                gated(NK - 1, 1, NT - 1, 3, NT - 3)
                v.wait_ge(tiles_used, l * NT + NT)
                for hf in range(2):
                    for t in range(TT):
                        v.tensor_copy(x[:, t, hf * HALF_N:(hf + 1) * HALF_N], acc[2 * t + hf][:, :]).then_inc(x_ready, 1)
                v.wait_ge(x_ready, l * 4 + 8)
                assert links[0] == NCHAIN + 1, links[0]
            v.wait_ge(root_ready, 3 * DEPTH + 1)
            v.reciprocal(stat[:, 4:6], stat[:, 2:4]).then_inc(rstd_ready, 1)
            v.wait_ge(fgain_loaded, 16)
            v.wait_ge(rstd_ready, 3 * DEPTH + 1)
            for t in range(TT):
                v.scalar_tensor_tensor(x[:, t, :], x[:, t, :], stat[:, 4 + t:5 + t], ring[:, 0, :], ALU.mult, ALU.mult)\
                    .then_inc(out_ready, 1)

        @block.tensor
        def _(pe):
            pe.sem_inc(outer_done, STEPS)
            pe.wait_ge(consts_loaded, 16)
            pe.wait_ge(rel_loaded, 32)
            pe.wait_ge(rel_low, 1)
            pe.matmul(bank[0][0:HEADS, 0:NDIST], relx, oh, start=True, stop=True).then_inc(rel_product, 1)
            pe.wait_ge(rel_vector, 1)

            with pe.Fori(0, DEPTH) as l:
                g = [0]

                def group(name):
                    assert PLAN[g[0]][0] == name, (PLAN[g[0]], name)
                    prev = last_in_bank(g[0])
                    if prev is not None:
                        tv, ta = taken_before(prev + 1)
                        if PLAN[prev][1] == "V":
                            pe.wait_ge(taken_v, l * NGV + tv)
                        else:
                            pe.wait_ge(taken_a, l * NGA + ta)
                    g[0] += 1
                    return bank[bank_of(g[0] - 1)]

                def tile(n, k):
                    pe.wait_ge(lo_pool, l * LOP + n + 2)
                    return halves[:, n % RING].rearrange("p h (k c) -> p h k c", k=k)

                def product(o, stationary, moving, begin=True, end=True):
                    for n, (a, b) in enumerate(TERMS):
                        i = pe.matmul(o, stationary[a], moving[b], start=begin and n == 0, stop=end and n == len(TERMS) - 1)
                        first_of = i if n == 0 else first_of
                    return first_of, i

                def columns(n, o, second=None):
                    w = tile(n, KD)
                    for k in range(KD):
                        if second is not None and k == KD // 2:
                            pe.wait_ge(scaled, second)
                        one, i = product(o, (w[:, 0, k], w[:, 1, k]), (hT[:, 0, k], hT[:, 1, k]), k == 0, k == KD - 1)
                        if k == 0:
                            one.then_inc(tiles_used, 1)
                    return i

                def transpose_rows(name):
                    for n in range(2):
                        for t in range(TT):
                            b = group(name)
                            for k in range(4):
                                i = pe.matmul(b[:, k * P:(k + 1) * P], x[:, t, (4 * n + k) * P:(4 * n + k + 1) * P],
                                              diag[:, t, :], start=True, stop=True)
                            i.then_inc(groups_done, 1)

                pe.wait_ge(params_ready, l + 1)
                pe.sem_inc(tiles_used, 1)
                pe.wait_ge(diag_ready, l * 2 + 1)
                transpose_rows("h1T")
                pe.wait_ge(scaled, l * 4 + 1)
                for n in range(QC // 2):
                    b = group("q")
                    for c in range(2):
                        i = columns(T_Q + 2 * n + c, b[:, c * S:(c + 1) * S], l * 4 + 2 if n + c == 0 else None)
                    i.then_inc(groups_done, 1)
                b = group("kv")
                columns(T_K, b[:, 0:S])
                w = tile(T_V, KD)
                for t in range(TT):
                    for k in range(KD):
                        rows = [hT[:, c, k, t * P:(t + 1) * P] for c in range(2)]
                        one, i = product(b[:, S + t * P:S + (t + 1) * P], rows, (w[:, 0, k], w[:, 1, k]), k == 0, k == KD - 1)
                        if t == 0 and k == 0:
                            one.then_inc(tiles_used, 1)
                i.then_inc(groups_done, 1)
                pe.wait_ge(taken_a, l * NGA + 3)
                for blk, per in ((0, 4), (1, 2)):
                    width = (blk + 1) * P
                    for n in range(HEADS // per):
                        b = group(f"lg{blk}")
                        for u in range(per):
                            h = per * n + u
                            rows = slice(0, HD) if h < 4 else slice(HD, P)
                            i = pe.matmul(b[:, u * width:(u + 1) * width], qT[rows, h % 4, blk * P:(blk + 1) * P],
                                          kT[rows, 0:width], start=True, stop=True)
                        i.then_inc(groups_done, 1)
                for name, t0 in (("pz", T_PZ), ("gu", T_GU)):
                    for n in range(GROUPS // 2):
                        b = group(name)
                        for c in range(2):
                            i = columns(t0 + 2 * n + c, b[:, c * S:(c + 1) * S])
                        i.then_inc(groups_done, 1)
                pe.wait_ge(probs_ready, l * 2 + 1)
                for n in range(2):
                    b = group("pT0")
                    for u in range(4):
                        i = pe.transpose(b[:, u * P:(u + 1) * P], lg0[:, 4 * n + u, :], ident)
                    i.then_inc(groups_done, 1)
                pe.wait_ge(probs_ready, l * 2 + 2)
                for n in range(4):
                    b = group("pT1")
                    for u in range(4):
                        i = pe.transpose(b[:, u * P:(u + 1) * P], lg1[:, 2 * n + u // 2, (u % 2) * P:(u % 2 + 1) * P], ident)
                    i.then_inc(groups_done, 1)
                pe.wait_ge(diff_ready, l + 1)
                for n in range(2):
                    b = group("pool")
                    for c in range(2):
                        gg = 2 * n + c
                        i = pe.matmul(b[:, c * S:(c + 1) * S], par[:, C_WPOOL + gg * P:C_WPOOL + (gg + 1) * P], dT[:, gg, :],
                                      start=True, stop=True)
                    i.then_inc(groups_done, 1)
                b = [group("gv") for _ in range(TT)]
                for c in range(2):
                    for kh in range(2):
                        w = tile(T_GV + 2 * c + kh, 4)
                        for t in range(TT):
                            for k in range(4):
                                rows = [hT[:, e, 4 * kh + k, t * P:(t + 1) * P] for e in range(2)]
                                one, i = product(b[t][:, c * S:(c + 1) * S], rows, (w[:, 0, k], w[:, 1, k]),
                                                 kh == 0 and k == 0, kh == 1 and k == 3)
                                if t == 0 and k == 0:
                                    one.then_inc(tiles_used, 1)
                            if c == 1 and kh == 1:
                                i.then_inc(groups_done, 1)
                pe.wait_ge(taken_a, l * NGA + taken_before(first("gv"))[1])
                for c in range(QC):
                    b = group("attn")
                    for u in range(2):
                        h = c + 4 * u
                        pe.matmul(b[:, u * S:u * S + P], v_tok[:, 0, :], pT0[:, h, :], start=True, stop=True)
                        for sblk in range(2):
                            i = pe.matmul(b[:, u * S + P:(u + 1) * S], v_tok[:, sblk, :], pT1[:, 2 * h + sblk, :],
                                          start=sblk == 0, stop=sblk == 1)
                    i.then_inc(groups_done, 1)
                pe.wait_ge(vhat_ready, l + 1)
                pe.wait_ge(wsp_ready, l + 1)
                for n in range(2):
                    b = group("gmlp")
                    for c in range(2):
                        gg = 2 * n + c
                        for t in range(TT):
                            i = pe.matmul(b[:, c * S + t * P:c * S + (t + 1) * P], gv[:, t, gg * P:(gg + 1) * P],
                                          wsp[:, gg, :], start=True, stop=True)
                    i.then_inc(groups_done, 1)
                pe.wait_ge(taken_a, l * NGA + taken_before(first("gate"))[1])
                for hf in range(2):
                    for br, mixed in enumerate(mixed_h):
                        t0 = T_MIX + hf * MIX_HALF + br * 6
                        for n in range(2):
                            b = group("gate")
                            for c in range(2):
                                i = columns(t0 + 2 * n + c, b[:, c * S:(c + 1) * S])
                            i.then_inc(groups_done, 1)
                        if hf == 0:
                            pe.wait_ge(mixed_ready, l * BR + br + 1)
                        for n in range(2):
                            b = group("branch")
                            w = tile(t0 + 4 + n, 4)
                            for c in range(2):
                                for k in range(4):
                                    part_w = [w[:, e, k, c * P:(c + 1) * P] for e in range(2)]
                                    one, i = product(b[:, c * S:(c + 1) * S], part_w, (mixed[:, 0, k], mixed[:, 1, k]),
                                                     k == 0, k == 3)
                                    if c == 0 and k == 0:
                                        one.then_inc(tiles_used, 1)
                            i.then_inc(groups_done, 1)
                for hf in range(2):
                    b = [group("wo") for _ in range(TT)]
                    for kq in range(4):
                        w = tile(T_WO + 4 * hf + kq, 2)
                        if hf == 0:
                            pe.wait_ge(merged_ready, l * 4 + kq + 1)
                        for t in range(TT):
                            for k in range(2):
                                rows = [merged_h[:, e, 2 * kq + k, t * P:(t + 1) * P] for e in range(2)]
                                one, i = product(b[t][:, :], rows, (w[:, 0, k], w[:, 1, k]), kq == 0 and k == 0,
                                                 kq == 3 and k == 1)
                                if t == 0 and k == 0:
                                    one.then_inc(tiles_used, 1)
                            if kq == 3:
                                i.then_inc(groups_done, 1)
                pe.wait_ge(taken_v, l * NGV + taken_before(first("h2T"))[0])
                for t in range(TT):
                    for hf in range(2):
                        pe.matmul(acc[2 * t + hf][:, :], ident, x[:, t, hf * HALF_N:(hf + 1) * HALF_N], start=True,
                                  stop=True)
                pe.wait_ge(diag_ready, l * 2 + 2)
                transpose_rows("h2T")
                pe.wait_ge(scaled, l * 4 + 3)
                for h in range(PH):
                    b = group("qq")
                    for c in range(2):
                        i = columns(T_WQ + 2 * h + c, b[:, c * S:(c + 1) * S], l * 4 + 4 if h + c == 0 else None)
                    i.then_inc(groups_done, 1)
                pe.wait_ge(taken_a, l * NGA + taken_before(first("score"))[1])
                for n in range(8):
                    b = group("score")
                    for u in range(2):
                        for c in range(2):
                            h, t = 2 * (n % 4) + u, n // 4
                            i = pe.matmul(b[:, (2 * u + c) * NK:(2 * u + c + 1) * NK], qqT[:, h, c, t * P:(t + 1) * P],
                                          par[:, C_SK + c * NK:C_SK + (c + 1) * NK], start=True, stop=True)
                    i.then_inc(groups_done, 1)
                def u_product(s, k, opens=False, chunks=range(KD)):
                    w = halves[:, s].rearrange("p h (k c) -> p h k c", k=KD)
                    for c in chunks:
                        one, i = product(bank_u[k][:, 0:S], (w[:, 0, c], w[:, 1, c]), (hT[:, 0, c], hT[:, 1, c]), c == 0,
                                         c == KD - 1)
                        if opens and c == 0:
                            one.then_inc(tiles_used, 1)
                    if chunks[-1] == KD - 1:
                        i.then_inc(tiles_used, 1)

                def v_product(b, s, k):
                    pe.wait_ge(lo_vector, l * NK + b + 2)
                    pe.wait_ge(coef_ready, l * NK + b + 1)
                    for t in range(TT):
                        for a, e in TERMS:
                            for hf in range(2):
                                i = pe.matmul(acc[2 * t + hf][:, :], coef[:, k, a, t * P:(t + 1) * P],
                                              halves[:, s, e, hf * HALF_N:(hf + 1) * HALF_N], start=False, stop=True,
                                              skip_group_check=True)
                    i.then_inc(tiles_used, 1)

                pe.wait_ge(taken_a, l * NGA + NGA - 2)
                for s in range(RING):
                    pe.wait_ge(lo_pool, l * LOP + (T_EU + s + 2))
                    if s >= 2:
                        pe.wait_ge(act_done, l * NK + (s - 1))
                    u_product(s, s % 2, opens=s == 0)

                def u_early(r, s):
                    pe.wait_ge(lo_pool, l * LOP + r * RING + (T_EU + s + 2))
                    pe.wait_ge(act_done, l * NK + r * RING + (s - 1))
                    u_product(s, s % 2)

                with pe.Fori(1, AT_SEARCH // RING - 1) as r:
                    for s in range(RING):
                        u_early(r, s)
                for s in range(RING):
                    if s == RING - 1:
                        pe.wait_ge(sel_ready, l + 1)
                        for t in range(TT):
                            b = group("sel")
                            for c in range(3):
                                i = pe.transpose(b[:, c * P:(c + 1) * P], sel[:, c, t, :], ident)
                            i.then_inc(groups_done, 1)
                        assert g[0] == NG
                    u_early(AT_SEARCH // RING - 1, s)

                with pe.Fori(0, NQ // BODY) as j:
                    for q in range(BODY):
                        s, g4 = q % STEPS, q // 2
                        pe.wait_ge(onehots_ready, l * NQ + j * BODY + (q + 1))
                        if q % 2:
                            pe.wait_ge(onehot_ready, l * NG4 + j * (BODY // 2) + (q // 2 + 1))
                        if q % 2 == 0:
                            pe.wait_ge(table_ready, l * NG4 + j * (BODY // 2) + (g4 + 1))
                        for u in range(2):
                            o = (2 * q + u) % 4 * NK
                            i = pe.matmul(bank_g[g4 % 2][:, o:o + NK], onehot1[:, s, u, :], onehot2[:, s, u, :],
                                          start=True, stop=True)
                        i.then_inc(outer_done, 1)
                        if q % 2 == 0:
                            continue
                        block_of, c = q // KD, q % KD - 1
                        if c == 0:
                            pe.wait_ge(lo_pool, l * LOP + j * PER + (T_TU + block_of + 2))
                            pe.wait_ge(act_done, l * NK + j * PER + (AT_SEARCH + block_of - 1))
                        u_product(block_of, block_of % 2, chunks=[c, c + 1])

                with pe.Fori(0, EARLY // RING) as r:
                    for s in range(RING):
                        v_product(r * RING + s, s, s % 2)

                def u_main(b, s, k):
                    pe.wait_ge(lo_pool, l * LOP + b + (T_EV - EARLY + 2))
                    pe.wait_ge(act_done, l * NK + b - 1)
                    u_product(s, k)

                u_main(EARLY, 0, 0)
                with pe.Fori(0, MAIN // 2 - 1) as r:
                    u_main(r * 2 + (EARLY + 1), 1, 1)
                    v_product(r * 2 + EARLY, 2, 0)
                    u_main(r * 2 + (EARLY + 2), 3, 0)
                    v_product(r * 2 + (EARLY + 1), 0, 1)
                u_main(NK - 1, 1, 1)
                v_product(NK - 2, 2, 0)
                v_product(NK - 1, 3, 1)


def shape_constants():
    c = np.zeros((P, K_END), np.float32)
    c[:, K_ID:K_ID + P] = np.eye(P)
    c[:, K_IOTA:K_IOTA + P] = np.arange(P)
    for g, w in enumerate(POOL_WINDOWS):
        c[:, K_CINV + g * S:K_CINV + (g + 1) * S] = 1.0 / np.minimum(np.arange(1, S + 1), w)
    c[:, K_TRIL:K_TRIL + P] = np.triu(np.ones((P, P)))
    exact = BUCKETS // 2
    for j in range(NDIST):
        dist = 2 * P - 1 - j
        if dist >= WINDOW or dist < 0:
            b = BUCKETS
        elif dist < exact:
            b = dist
        else:
            b = min(BUCKETS - 1, exact + int(np.log(dist / exact) / np.log(MAX_DIST / exact) * (BUCKETS - exact)))
        c[b, K_OH + j] = 1.0
    return c


def lay_out(inp):
    w_in = inp["w_in"]
    n_q, n_kv = HEADS * HD, 2 * HD
    order = np.concatenate([np.r_[c * HD:(c + 1) * HD, (c + 4) * HD:(c + 5) * HD] for c in range(QC)])
    out = np.zeros((DEPTH, NT, P, TILE), np.float32)

    def cols(w, c0, n):
        return w[:, c0:c0 + n * P].reshape(KD, P, n, P).transpose(2, 1, 0, 3).reshape(n, P, TILE)

    for l in range(DEPTH):
        o, w = out[l], w_in[l]
        par = np.zeros((P, 2 * TILE), np.float32)
        par[:, C_SK:C_SK + NK] = inp["peer_sub_keys1"][l].T
        par[:, C_SK + NK:C_SK + 2 * NK] = inp["peer_sub_keys2"][l].T
        par[:, C_WPOOL:C_WPOOL + GROUPS * P] = inp["w_pool"][l].transpose(1, 0, 2).reshape(P, -1)
        par[:, C_WSP:C_WSP + GROUPS * P] = inp["w_spatial"][l].transpose(2, 0, 1).reshape(P, -1)
        for c, name, k in ((C_AGAIN, "attn_norm_gain", KD), (C_FGAIN, "ffn_norm_gain", KD), (C_BGATE, "b_gate", BR * KD),
                           (C_PSCALE, "pool_scale", GROUPS), (C_VGAIN, "gmlp_v_gain", GROUPS)):
            par[:, c:c + k] = inp[name][l].reshape(k, P).T
        par[:, C_SINK:C_SINK + HEADS] = inp["attn_sinks"][l][None]
        par[:, C_BSP:C_BSP + GROUPS * P] = inp["b_spatial"][l].reshape(1, -1)
        o[T_PARAM:T_Q] = par.reshape(P, 2, TILE).transpose(1, 0, 2)
        o[T_Q:T_K] = cols(w[:, order], 0, QC)
        o[T_K:T_PZ] = cols(w, n_q, 2)
        c0 = n_q + 2 * n_kv
        o[T_PZ:T_GU] = cols(w, c0, GROUPS)
        o[T_GU:T_GV] = cols(w, c0 + GROUPS * P, GROUPS)
        c0 += 2 * GROUPS * P
        o[T_GV:T_MIX] = w[:, c0:c0 + GROUPS * P].reshape(2, 4, P, 2, S).transpose(3, 0, 2, 1, 4).reshape(4, P, TILE)
        c0 += GROUPS * P
        branch = (inp["w_branch_a"][l][order], inp["w_branch_b"][l], inp["w_branch_c"][l])
        for hf in range(2):
            for br in range(BR):
                t0 = T_MIX + hf * MIX_HALF + br * 6
                o[t0:t0 + 4] = cols(w, c0 + br * D + hf * HALF_N, 4)
                wb = branch[br][:, hf * HALF_N:(hf + 1) * HALF_N]
                o[t0 + 4:t0 + 6] = wb.reshape(4, P, 2, S).transpose(2, 1, 0, 3).reshape(2, P, TILE)
        o[T_WO:T_WQ] = inp["w_out"][l].reshape(4, 2, P, 2, HALF_N).transpose(3, 0, 2, 1, 4).reshape(8, P, TILE)
        o[T_WQ:T_EU] = cols(inp["peer_w_query"][l], 0, 2 * PH)
        u = inp["peer_expert_u"][l].reshape(NK, NK, KD, P)
        v = inp["peer_expert_v"][l].reshape(NK, NK, D)
        u = u.transpose(1, 3, 2, 0).reshape(NK, P, TILE)
        v = v.transpose(1, 0, 2)
        o[T_EU:T_EV] = u[:EARLY]
        o[T_EV:T_EV + 2] = v[EARLY - 2:EARLY]
        o[T_EV + 2:T_MU] = v[:EARLY - 2]
        o[T_MU] = u[EARLY]
        o[T_MU + 1:NT - 1:2] = u[EARLY + 1:]
        o[T_MU + 2:NT - 1:2] = v[EARLY:-1]
        o[NT - 1] = v[-1]
    return out.reshape(DEPTH * NT, P, TILE)


def kernel(**inputs):
    import concourse.bacc as bacc
    from concourse.bass_utils import run_bass_kernel_spmd

    inp = {k: np.ascontiguousarray(a) for k, a in inputs.items()}
    arrays = {
        "x": inp["x"],
        "stream": lay_out(inp),
        "consts": shape_constants(),
        "rel_bias": inp["rel_bias"],
        "final_gain": np.ascontiguousarray(np.broadcast_to(inp["final_gain"][None], (P, D))),
    }
    nc = bacc.Bacc("TRN2", target_bir_lowering=False, num_devices=1)
    args = [nc.dram_tensor(f"in_{n}", a.shape, mybir.dt.from_np(a.dtype), kind="ExternalInput").ap()
            for n, a in arrays.items()]
    out = nc.dram_tensor("out_y", (1, S, D), F32, kind="ExternalOutput").ap()
    program(nc, *args, out)
    r = run_bass_kernel_spmd(nc, [{f"in_{n}": a for n, a in arrays.items()}], core_ids=[0])
    return r.results[0]["out_y"]
```
